# Optimizing a Trainium2 kernel written in Bass

```python
import jax, jax.numpy as jnp
from jax import lax
import numpy as np

D_MODEL = 1024
BATCH = 1
SEQ = 1024
DEPTH = 2

N_A_LAYERS = DEPTH // 2
N_B_LAYERS = DEPTH - N_A_LAYERS
MEM_TOKENS = 256
MEM_HEADS = 4
MEM_HEAD_DIM = 64
MEM_WIDTH = MEM_HEADS * MEM_HEAD_DIM
CONV_CH = D_MODEL - MEM_WIDTH
CONV_WIDTH = 31
MIX_WIDTH_A = CONV_CH + MEM_WIDTH
SB_HEADS = 4
SB_HEAD_DIM = 128
SB_WIDTH = SB_HEADS * SB_HEAD_DIM
MIX_WIDTH_B = SB_WIDTH + MEM_WIDTH
Q_BLOCK = 128
N_GROUPS = 4
EXPERTS_PER_GROUP = 4
EXPERT_TOP_K = 2
EXPERT_HIDDEN = D_MODEL // 8
EPS = 1e-6

kernel_name = "yoco_conformer_stickbreak_hmoe"

def rms_norm(x, g):
    xf = x.astype(jnp.float32)
    y = xf * lax.rsqrt(jnp.mean(xf * xf, axis=-1, keepdims=True) + EPS)
    return (y * g.astype(jnp.float32)).astype(x.dtype)

def layer_norm(x, g, b):
    xf = x.astype(jnp.float32)
    xc = xf - jnp.mean(xf, axis=-1, keepdims=True)
    var = jnp.mean(xc * xc, axis=-1, keepdims=True)
    y = xc * lax.rsqrt(var + EPS) * g.astype(jnp.float32) + b.astype(jnp.float32)
    return y.astype(x.dtype)

def split_heads(x, n_heads, head_dim):
    b, s, _ = x.shape
    return x.reshape(b, s, n_heads, head_dim).transpose(0, 2, 1, 3)

def merge_heads(x):
    b, h, s, d = x.shape
    return x.transpose(0, 2, 1, 3).reshape(b, s, h * d)

def conformer_conv(u, conv_w, ln_g, ln_b):
    a, gate = jnp.split(u, 2, axis=-1)
    c = a * jax.nn.sigmoid(gate)
    c = lax.conv_general_dilated(
        c, conv_w.astype(c.dtype)[:, None, :], window_strides=(1,),
        padding=[(CONV_WIDTH - 1, 0)], dimension_numbers=("NWC", "WIO", "NWC"),
        feature_group_count=CONV_CH)
    c = layer_norm(c, ln_g, ln_b)
    return jax.nn.silu(c)

def memory_attention(q, mem_k, mem_v, q_g):
    qh = rms_norm(split_heads(q, MEM_HEADS, MEM_HEAD_DIM), q_g).astype(jnp.float32)
    s = jnp.einsum("bhsd,bhmd->bhsm", qh, mem_k.astype(jnp.float32)) * (MEM_HEAD_DIM ** -0.5)
    p = jax.nn.softmax(s, axis=-1)
    o = jnp.einsum("bhsm,bhmd->bhsd", p, mem_v.astype(jnp.float32))
    return merge_heads(o).astype(q.dtype)

def stick_breaking_attention(q, k, v):
    b, h, seq, _ = q.shape
    n_blocks = seq // Q_BLOCK
    scale = SB_HEAD_DIM ** -0.5
    idx = jnp.arange(Q_BLOCK)
    diag_mask = idx[None, :] < idx[:, None]
    u_rev = jnp.asarray(np.tri(Q_BLOCK, Q_BLOCK, 0, dtype=np.float32))
    kf = k.astype(jnp.float32)
    vf = v.astype(jnp.float32)
    outs = []
    for i in range(n_blocks):
        n_k = i + 1
        n_keys = n_k * Q_BLOCK
        qb = q[:, :, i * Q_BLOCK:(i + 1) * Q_BLOCK].astype(jnp.float32)
        z = jnp.einsum("bhqd,bhkd->bhqk", qb, kf[:, :, :n_keys]) * scale
        mask = jnp.concatenate(
            [jnp.ones((Q_BLOCK, n_keys - Q_BLOCK), bool), diag_mask], axis=1)
        lf = jnp.where(mask, jax.nn.log_sigmoid(-z), 0.0)
        lf = lf.reshape(b, h, Q_BLOCK, n_k, Q_BLOCK)
        within = jnp.einsum("bhqnk,kj->bhqnj", lf, u_rev)
        later_tri = jnp.asarray(np.tri(n_k, n_k, -1, dtype=np.float32))
        later = jnp.einsum("bhqn,nm->bhqm", jnp.sum(lf, axis=-1), later_tri)
        rev = (within + later[..., None]).reshape(b, h, Q_BLOCK, n_keys)
        w = jnp.exp(jnp.where(mask, z + rev, -jnp.inf))
        outs.append(jnp.einsum("bhqk,bhkd->bhqd", w, vf[:, :, :n_keys]))
    out = jnp.concatenate(outs, axis=2)
    return merge_heads(out).astype(q.dtype)

def hier_moe(h, rg_w, rg_b, re_w, re_b, w_in, w_down):
    b, s, d = h.shape
    t = h.reshape(-1, d)
    tf = t.astype(jnp.float32)
    group_logits = tf @ rg_w.astype(jnp.float32) + rg_b.astype(jnp.float32)
    group_prob = jax.nn.softmax(group_logits, axis=-1)
    g_idx = jnp.argmax(group_logits, axis=-1)
    g_onehot = jax.nn.one_hot(g_idx, N_GROUPS, dtype=jnp.float32)
    g_gate = jnp.max(group_prob, axis=-1, keepdims=True)
    exp_logits = jnp.einsum("td,gde->tge", tf, re_w.astype(jnp.float32)) + re_b.astype(jnp.float32)
    sel_logits = jnp.einsum("tge,tg->te", exp_logits, g_onehot)
    top_v, top_i = lax.top_k(sel_logits, EXPERT_TOP_K)
    top_w = jax.nn.softmax(top_v, axis=-1) * g_gate
    expert_gate = jnp.sum(jax.nn.one_hot(top_i, EXPERTS_PER_GROUP, dtype=jnp.float32)
                          * top_w[..., None], axis=1)
    gate = g_onehot[:, :, None] * expert_gate[:, None, :]
    y = jnp.zeros(t.shape, jnp.float32)
    for g in range(N_GROUPS):
        hu = jnp.einsum("td,edf->tef", t, w_in[g])
        a, u = jnp.split(hu, 2, axis=-1)
        act = jax.nn.silu(a) * u * gate[:, g, :, None].astype(hu.dtype)
        y = y + jnp.einsum("teh,ehd->td", act, w_down[g]).astype(jnp.float32)
    return y.reshape(b, s, d).astype(h.dtype)

def setup_inputs(seed: int = 0) -> dict:
    key = jax.random.key(seed)
    ks = jax.random.split(key, 25)
    f32 = jnp.float32

    def nrm(k, shape, scale):
        return jax.random.normal(k, shape, f32) * scale

    def gain(k, shape):
        return 1.0 + 0.02 * jax.random.normal(k, shape, f32)

    n_a, n_b = N_A_LAYERS, N_B_LAYERS
    return {
        "x": nrm(ks[0], (BATCH, SEQ, D_MODEL), 1.0),
        "mem": nrm(ks[1], (BATCH, MEM_TOKENS, D_MODEL), 1.0),
        "mem_norm_g": gain(ks[2], (D_MODEL,)),
        "mix_norm_g": gain(ks[3], (DEPTH, D_MODEL)),
        "ffn_norm_g": gain(ks[4], (DEPTH, D_MODEL)),
        "w_in_a": nrm(ks[5], (n_a, D_MODEL, 2 * CONV_CH + MEM_WIDTH), D_MODEL ** -0.5),
        "conv_w": nrm(ks[6], (n_a, CONV_WIDTH, CONV_CH), CONV_WIDTH ** -0.5),
        "conv_ln_g": gain(ks[7], (n_a, CONV_CH)),
        "conv_ln_b": nrm(ks[8], (n_a, CONV_CH), 0.02),
        "w_out_a": nrm(ks[9], (n_a, MIX_WIDTH_A, D_MODEL), 0.5 * MIX_WIDTH_A ** -0.5),
        "w_in_b": nrm(ks[10], (n_b, D_MODEL, SB_WIDTH + MEM_WIDTH), D_MODEL ** -0.5),
        "sb_q_norm_g": gain(ks[11], (n_b, SB_HEAD_DIM)),
        "w_out_b": nrm(ks[12], (n_b, MIX_WIDTH_B, D_MODEL), 0.5 * MIX_WIDTH_B ** -0.5),
        "kv_norm_g": gain(ks[13], (D_MODEL,)),
        "w_kv": nrm(ks[14], (D_MODEL, 2 * SB_WIDTH), D_MODEL ** -0.5),
        "sb_k_norm_g": gain(ks[15], (SB_HEAD_DIM,)),
        "w_mem_kv": nrm(ks[16], (DEPTH, D_MODEL, 2 * MEM_WIDTH), D_MODEL ** -0.5),
        "mem_q_norm_g": gain(ks[17], (DEPTH, MEM_HEAD_DIM)),
        "mem_k_norm_g": gain(ks[18], (DEPTH, MEM_HEAD_DIM)),
        "router_g_w": nrm(ks[19], (DEPTH, D_MODEL, N_GROUPS), D_MODEL ** -0.5),
        "router_g_b": nrm(ks[20], (DEPTH, N_GROUPS), 0.01),
        "router_e_w": nrm(ks[21], (DEPTH, N_GROUPS, D_MODEL, EXPERTS_PER_GROUP), D_MODEL ** -0.5),
        "router_e_b": nrm(ks[22], (DEPTH, N_GROUPS, EXPERTS_PER_GROUP), 0.01),
        "moe_w_in": nrm(ks[23], (DEPTH, N_GROUPS, EXPERTS_PER_GROUP, D_MODEL, 2 * EXPERT_HIDDEN), D_MODEL ** -0.5),
        "moe_w_down": nrm(ks[24], (DEPTH, N_GROUPS, EXPERTS_PER_GROUP, EXPERT_HIDDEN, D_MODEL), EXPERT_HIDDEN ** -0.5),
    }

def reference(x, mem, mem_norm_g, mix_norm_g, ffn_norm_g, w_in_a, conv_w, conv_ln_g, conv_ln_b,
              w_out_a, w_in_b, sb_q_norm_g, w_out_b, kv_norm_g, w_kv, sb_k_norm_g, w_mem_kv,
              mem_q_norm_g, mem_k_norm_g, router_g_w, router_g_b, router_e_w, router_e_b,
              moe_w_in, moe_w_down):
    mem_n = rms_norm(mem, mem_norm_g)
    sb_k = None
    sb_v = None
    for l in range(DEPTH):
        h = rms_norm(x, mix_norm_g[l])
        mk, mv = jnp.split(mem_n @ w_mem_kv[l], 2, axis=-1)
        mk = rms_norm(split_heads(mk, MEM_HEADS, MEM_HEAD_DIM), mem_k_norm_g[l])
        mv = split_heads(mv, MEM_HEADS, MEM_HEAD_DIM)
        if l < N_A_LAYERS:
            u = h @ w_in_a[l]
            glu_in, q_mem = u[..., :2 * CONV_CH], u[..., 2 * CONV_CH:]
            mixed = conformer_conv(glu_in, conv_w[l], conv_ln_g[l], conv_ln_b[l])
            w_out = w_out_a[l]
        else:
            j = l - N_A_LAYERS
            u = h @ w_in_b[j]
            q_sb, q_mem = u[..., :SB_WIDTH], u[..., SB_WIDTH:]
            q_sb = rms_norm(split_heads(q_sb, SB_HEADS, SB_HEAD_DIM), sb_q_norm_g[j])
            mixed = stick_breaking_attention(q_sb, sb_k, sb_v)
            w_out = w_out_b[j]
        mem_out = memory_attention(q_mem, mk, mv, mem_q_norm_g[l])
        x = x + jnp.concatenate([mixed.astype(x.dtype), mem_out.astype(x.dtype)], axis=-1) @ w_out
        x = x + hier_moe(rms_norm(x, ffn_norm_g[l]), router_g_w[l], router_g_b[l],
                         router_e_w[l], router_e_b[l], moe_w_in[l], moe_w_down[l])
        if l == N_A_LAYERS - 1:
            s = rms_norm(x, kv_norm_g)
            k_all, v_all = jnp.split(s @ w_kv, 2, axis=-1)
            sb_k = rms_norm(split_heads(k_all, SB_HEADS, SB_HEAD_DIM), sb_k_norm_g)
            sb_v = split_heads(v_all, SB_HEADS, SB_HEAD_DIM)
    return x


_drawn_inputs = setup_inputs


def setup_inputs(seed=0):
    import zlib

    import numpy as np

    out = dict(_drawn_inputs(seed))
    spreads = {}
    factors = {'mem_norm_g': 8.0,
     'mix_norm_g': 2.948,
     'conv_ln_b': 2.67,
     'sb_q_norm_g': 6.098,
     'kv_norm_g': 4.382,
     'sb_k_norm_g': 5.515,
     'mem_q_norm_g': 8.0,
     'mem_k_norm_g': 8.0,
     'router_g_b': 4.481,
     'router_e_b': 3.387}
    for name, (base, spread) in spreads.items():
        noise = np.random.default_rng([zlib.crc32(name.encode()), seed]).standard_normal(out[name].shape)
        drawn = base * np.exp(spread * noise) if base else spread * noise
        out[name] = __import__('jax').numpy.asarray(drawn.astype(out[name].dtype))
    for name, factor in factors.items():
        out[name] = (out[name] * factor).astype(out[name].dtype)
    return out
```

```python
from contextlib import ExitStack

import numpy as np

import concourse.bass as bass
from concourse import mybir

F32 = mybir.dt.float32
F32R = mybir.dt.float32r
BF16 = mybir.dt.bfloat16
I32 = mybir.dt.int32
ALU = mybir.AluOpType
ACT = mybir.ActivationFunctionType
AX = mybir.AxisListType.X

P = 128
D = 1024
T = 1024
TT = T // P
KT = D // P
MEM = 256
MT = MEM // P
MH, MHD = 4, 64
MW = MH * MHD
CC = D - MW
CT = CC // P
CW = 31
SH, SHD = 4, 128
SW = SH * SHD
G, EPG, HID = 4, 4, 128
EPS = 1e-6
WC = 256
MTILE = 256
NMT = (T - G) // MTILE + G
NSUB = NMT * MTILE // P
NSTEP = NMT * EPG
BIG = 1.0e30

CHUNKS = [("mem", l, c) for l in range(2) for c in range(2)]
GLU_FIRST = 4
CHUNKS += [("glu", 0, c) for c in range(GLU_FIRST)] + [("qm", 0, 0)] + [("glu", 0, c) for c in range(GLU_FIRST, CT)]
CHUNKS += [("wo", 0, c) for c in range(4)]
_moe = lambda l: [("in", l, 0)] + [x for s in range(1, NSTEP) for x in (("in", l, s), ("dn", l, s - 1))] + [("dn", l, NSTEP - 1)]
CHUNKS += _moe(0)
CHUNKS += [("kv", 0, c) for c in (0, 2, 1, 3)] + [("qm", 1, 0), ("qs", 1, 0), ("qs", 1, 1)]
CHUNKS += [("wo", 1, c) for c in range(4)] + _moe(1)
CH = {k: n for n, k in enumerate(CHUNKS)}
RAW = 3
SLOT, PREV = [], []
RSLOT, RPREV = [], []
_last, _turn = {}, 0
for _n, (_kind, _l, _c) in enumerate(CHUNKS):
    _inmoe = _kind in ("in", "dn")
    _turn = (_turn + 1) % (3 if _inmoe else 2)
    SLOT.append(_turn)
    if _turn == 2 and (_kind, _c) in (("in", 0), ("in", 1), ("dn", 0)) and _last.get(2, -1) < CH[("wo", _l, 3)]:
        PREV.append(CH[("wo", _l, 3)])
    else:
        PREV.append(_last.get(_turn, -1))
    _last[_turn] = _n
_last, _turn = {}, 0
for _n, (_kind, _l, _c) in enumerate(CHUNKS):
    _turn = (_turn + 1) % (3 if _kind in ("in", "dn") else 2)
    RSLOT.append(_turn)
    RPREV.append(_last.get(_turn, -1))
    if _turn == 2 and _last.get(2, -1) < CH[("in", _l, 0)]:
        RPREV[-1] = -1
    _last[_turn] = _n
LO_P = [768 if k == "in" else 0 if k in ("dn", "kv", "qs") or (k, l) == ("qm", 1) else 2048 for k, l, _ in CHUNKS]
LO_P_CNT = [sum(x > 0 for x in LO_P[:n + 1]) for n in range(len(CHUNKS))]
LO_V_CNT = [sum(x < 2048 for x in LO_P[:n + 1]) for n in range(len(CHUNKS))]

JOBS = []


def _nt(name, tiles, lo):
    return [((name, t, h), lo) for t in range(tiles) for h in range(2)]


def _moe_jobs(l):
    out = [(("x", l, 0, h), True) for h in range(4)]
    for s in range(NSTEP + 1):
        i, e = divmod(s, EPG)
        if s < NSTEP and i + 1 < NMT:
            out.append((("x", l, i + 1, e), True))
        if s >= 1:
            out.append((("act", l, s - 1), True))
    return out


def _attn_jobs(l):
    out = []
    for t in range(TT + 1):
        if t < TT:
            out += [(("p", l, t, h), False) for h in range(2)]
        if t >= 1:
            out.append((("o", l, t - 1), True))
    return out


def _hn(name):
    return [((name, pr, h), False) for pr in range(2) for h in range(2)]


JOBS += [(("cw",), False)]
JOBS += _nt("nmem", MT, True) + [(("mk", 0), False), (("mk", 1), False)] + _nt("nmix0", TT, True)
JOBS += _hn("hm0") + _attn_jobs(0) + _nt("ffn0", TT, False) + _moe_jobs(0)
JOBS += _nt("nkv", TT, True) + _hn("hk0") + _hn("hk1")
JOBS += _hn("hm1") + _hn("hq0") + _attn_jobs(1) + _hn("hq1") + _nt("ffn1", TT, False) + _moe_jobs(1)
JOB = {k: n for n, (k, _) in enumerate(JOBS)}
JOB_LO = [sum(d for _, d in JOBS[:n + 1]) for n in range(len(JOBS))]

TILES = [(("mem", l, c, t), False) for l in range(2) for c in range(2) for t in range(MT)]
TILES += [(("qm", 0, 0, t), False) for t in range(TT)]
TILES += [(("wo", 0, c, t), True) for c in range(4) for t in range(TT)]
TILES += [(("kv", 0, c, t), False) for c in (0, 2, 1, 3) for t in range(TT)]
TILES += [(("qm", 1, 0, t), False) for t in range(TT)] + [(("qs", 1, c, t), False) for c in range(2) for t in range(TT)]
TILES += [(("wo", 1, c, t), True) for c in range(4) for t in range(TT)]
TILE = {k: n for n, (k, _) in enumerate(TILES)}
TILE_CNT = [sum(TILES[m][1] == TILES[n][1] for m in range(n + 1)) for n in range(len(TILES))]

SB_STEPS = []
for _b in range(TT - 1, -1, -1):
    for _h in (1, 0):
        _q0 = max(_b * P, _h * 512)
        if _q0 < (_h + 1) * 512:
            SB_STEPS.append((_b, _q0, (_h + 1) * 512 - _q0, _q0 == _b * P))
NSB = len(SB_STEPS)
LN_EXP_SET = 6
ZB = 4


def trunk(nc, a, out):
    ctx = ExitStack()
    with ctx:
        def sb(name, shape, dt=F32, stack=ctx):
            return stack.enter_context(nc.sbuf_tensor(name, shape, dt))

        sems = {}

        def sem(name):
            if name not in sems:
                sems[name] = ctx.enter_context(nc.semaphore(name))
            return sems[name]

        def region(name, *sets):
            t, most = {}, 0
            for tensors in sets:
                with ExitStack() as shelf:
                    for n, s, dt in tensors:
                        t[n] = sb(n, s, dt, shelf)
                most = max(most, sum(int(np.prod(s[1:])) * (2 if dt == BF16 else 4) for _, s, dt in tensors))
            sb(name, [P, -(-most // 4)])
            return t

        hn = [nc.dram_tensor(f"hn{l}", [T, D], F32).ap() for l in range(2)]
        ybuf = [nc.dram_tensor(f"ybuf{l}", [NSUB * P, D], F32).ap() for l in range(2)]
        xsave = nc.dram_tensor("xsave", [T, D], F32).ap()

        wraw_ = [sb(f"wraw{i}", [P, 2048]) for i in range(2)]
        whi_ = [sb(f"whi{i}", [P, 2048], F32R) for i in range(2)]
        wlo_ = [sb(f"wlo{i}", [P, 2048], F32R) for i in range(2)]
        hb = sb("hb", [P, 2048])
        gkv = sb("gkv", [P, KT])
        gmix1 = sb("gmix1", [P, KT])
        gb = sb("gb", [P, D])
        mkT = sb("mkT", [P, 2, 2, MEM])
        mv = sb("mv", [P, 2, MT, MW])
        junk = sb("junk", [P, D], BF16)
        ident = sb("ident", [P, P])
        ones = sb("ones", [P, P])
        nones = sb("nones", [P, P])
        nuinc = sb("nuinc", [P, P])
        lstrict = sb("lstrict", [P, P])
        negm = sb("negm", [P, P])
        iota = sb("iota", [P, P])
        tokid = sb("tokid", [P, TT])
        desc = sb("desc", [P, 4])
        iota_i = sb("iota_i", [P, P], I32)
        cw = sb("cw", [P, CT, CW + 2])
        gr = sb("gr", [8, P])
        gcol = sb("gcol", [P, 8])
        rw = sb("rw", [P, 5, KT, 4])
        rbias = sb("rbias", [P, 20])
        ssq = sb("ssq", [P, 32])
        rs = sb("rs", [P, 32])
        ssqx = sb("ssqx", [P, TT])
        rsx = sb("rsx", [P, TT])
        nx = sb("nx", [P, 32])
        ny = sb("ny", [P, 32])
        nt_ = sb("nt_", [P, 32])
        eps_t = sb("eps_t", [P, 1])
        mx = sb("mx", [P, TT, 4])
        nmx = sb("nmx", [P, TT, 4])
        psm = sb("psm", [P, TT, 4])
        pri = sb("pri", [P, TT, 4])
        idx = sb("idx", [P, NSUB], I32)
        slot_i = sb("slot_i", [P, TT], I32)
        gates = sb("gates", [P, NSUB, 4])
        grp = sb("grp", [P, 8], I32)
        A = region("region_a", [("hth_a", [P, 6, T], F32R), ("htl_a", [P, 6, T], F32R)],
                   [("xth", [P, 2, KT, MTILE], F32R), ("xtl", [P, 2, KT, MTILE], F32R), ("ath", [P, 2, 2 * P], F32R),
                    ("atl", [P, 2, 2 * P], F32R), ("xg", [P, 2, D], F32)],
                   [("yg", [P, TT, D], F32)])
        B = region("region_b", [("hth_b", [P, 2, T], F32R), ("htl_b", [P, 2, T], F32R)],
                   [("whi2", [P, 2048], F32R), ("wlo2", [P, 2048], F32R)],
                   [("lfsum", [P, 2, T], F32), ("wgt", [P, 2, 512], F32), ("on1", [P, 2, MW], F32)])
        C = region("region_c", [("X", [P, TT, D], F32)],
                   [("qmT0", [P, 2, T], F32), ("pb0", [P, 2, D], F32), ("pt0", [P, 2, D], F32), ("on0", [P, 2, MW], F32),
                    ("sg", [P, 2, 512], F32)],
                   [("qT", [P, SH, T], F32), ("qmT1", [P, 2, T], F32), ("hb2", [P, 2048], F32)],
                   [("pad_c", [P, SH, T], F32), ("lt", [P, 3, 512], F32), ("sp", [P, 3, 512], F32)])
        E = region("region_e", [("memb", [P, MT, D], F32), ("mth", [P, KT, MEM], F32R), ("mtl", [P, KT, MEM], F32R),
                    ("cwr", [CW + 2, CC], F32), ("mkraw", [P, 2, MT, MW], F32)],
                   [("cin", [P, 2, T + CW - 1], F32), ("cv", [P, CT, T], F32)],
                   [("kT", [P, SH, T], F32), ("V", [P, TT, SW], F32)],
                   [("sgm", [P, 2, 2, P], F32), ("actm", [P, 2, 2, P], F32), ("rt", [P, 8, 160], F32),
                    ("rT", [P, 2, KT, P], F32), ("boh", [P, TT, P], F32), ("av", [P, TT, NSUB, 5], F32)],
                   [("pad_e", [P, 2304], F32), ("ysb", [P, 2, 2, D], F32), ("wraw2", [P, 2048], F32)])
        X = C["X"]
        C["pb1"] = C["hb2"][:, 0:D].rearrange("p (o n) -> p o n", o=1)
        C["pt1"] = C["hb2"][:, D:2 * D].rearrange("p (o n) -> p o n", o=1)
        PS = ctx.enter_context(nc.psum_tensor("PS", [P, 8, 512], F32))

        def bank(n):
            return PS[:, n, :]

        def banks(n):
            return PS[:, n:n + 2, :].rearrange("p a b -> p (a b)")

        def whi(n):
            return whi_[SLOT[n]] if SLOT[n] < 2 else B["whi2"]

        def wlo(n):
            return wlo_[SLOT[n]] if SLOT[n] < 2 else B["wlo2"]

        def wraw(n):
            return wraw_[RSLOT[n]] if RSLOT[n] < 2 else E["wraw2"]

        def width(n):
            kind, l, _ = CHUNKS[n]
            return 1024 if kind == "dn" else 6 * WC if (kind, l) == ("wo", 1) else 2048

        def hth(k):
            return A["hth_a"][:, k, :] if k < 6 else B["hth_b"][:, k - 6, :]

        def htl(k):
            return A["htl_a"][:, k, :] if k < 6 else B["htl_b"][:, k - 6, :]

        def halves(name, t, h):
            tok = slice(t * P, t * P + P)
            if name == "nmem":
                return [(0, 4, E["mth"][:, 4 * h:4 * h + 4, tok], E["mtl"][:, 4 * h:4 * h + 4, tok])]
            if h == 0:
                return [(0, 4, A["hth_a"][:, 0:4, tok], A["htl_a"][:, 0:4, tok])]
            return [(0, 2, A["hth_a"][:, 4:6, tok], A["htl_a"][:, 4:6, tok]),
                    (2, 4, B["hth_b"][:, :, tok], B["htl_b"][:, :, tok])]

        w_raw = [sem(f"w_raw{i}") for i in range(RAW)]
        w_hi, w_lo_p, w_lo_v = sem("w_hi"), sem("w_lo_p"), sem("w_lo_v")
        xp_ready, xp_act, xp_dve = sem("xp_ready"), sem("xp_act"), sem("xp_dve")
        pj_ready, pj_a, pj_v = sem("pj_ready"), sem("pj_a"), sem("pj_v")
        v_step, a_step, p_step = sem("v_step"), sem("a_step"), sem("p_step")
        h_ready = sem("h_ready")
        NT_BASE = {"nmem": 0, "nmix0": MT, "ffn0": MT + TT, "nkv": MT + 2 * TT, "ffn1": MT + 3 * TT}
        SQ_BASE = {"nmem": 0, "nmix0": MT, "ffn0": MT + TT, "nkv": MT + 2 * TT, "ffn1": MT + 3 * TT}
        GB = {"nmem": 1, "nmix0": 2, "ffn0": 3, "ffn1": 4}
        HN = {"hm0": 0, "hk0": 1, "hk1": 2, "hm1": 3, "hq0": 4, "hq1": 5}
        HN_CHUNK = {"hm0": ("qm", 0, 0), "hk0": ("kv", 0, 0), "hk1": ("kv", 0, 1), "hq0": ("qs", 1, 0),
                    "hq1": ("qs", 1, 1), "hm1": ("qm", 1, 0)}

        HB_BEFORE = {"nmix0": ("nmem", MT - 1, 1), "ffn0": ("hm0", 1, 1), "nkv": ("ffn0", TT - 1, 1),
                     "ffn1": ("hq1", 1, 1)}

        def raw_heads(name):
            return C["hb2"] if name == "hq0" else hb

        def chunk_done(eng, n):
            kind, l, c = CHUNKS[n]
            if kind == "glu":
                eng.wait_ge(sem("glu_ready"), 2 * c + 2)
            elif kind == "in":
                eng.wait_ge(sem("hid_ready"), 2 * (l * NSTEP + c) + 2)
            elif kind == "dn":
                eng.wait_ge(sem("down_ready"), l * NSTEP + c + 1)
            else:
                eng.wait_ge(pj_ready, TILE[kind, l, c, (MT if kind == "mem" else TT) - 1] + 1)

        def weight_gain(n):
            kind, l, _ = CHUNKS[n]
            return gkv if kind == "kv" else gmix1 if l == 1 and kind in ("qm", "qs") else None

        def lo_made(eng, n):
            if LO_P[n]:
                eng.wait_ge(w_lo_p, LO_P_CNT[n])
            if LO_P[n] < 2048:
                eng.wait_ge(w_lo_v, LO_V_CNT[n])

        def tile_out(eng, key):
            eng.wait_ge(pj_v if TILES[TILE[key]][1] else pj_a, TILE_CNT[TILE[key]])

        def group_of(s):
            return s // EPG

        block = ctx.enter_context(nc.Block())

        @block.sync
        def _(sp):
            def weight_source(n, g=None):
                kind, l, c = CHUNKS[n]
                if kind == "mem":
                    return a["w_mem_kv"][l].rearrange("(p k) n -> p k n", k=KT)[:, :, c * WC:(c + 1) * WC]
                if kind == "qm":
                    w, at = (a["w_in_a"], 2 * CC) if l == 0 else (a["w_in_b"], SW)
                    return w[0].rearrange("(p k) n -> p k n", k=KT)[:, :, at:at + WC]
                if kind == "qs":
                    return a["w_in_b"][0].rearrange("(p k) n -> p k n", k=KT)[:, :, c * WC:(c + 1) * WC]
                if kind == "kv":
                    return a["w_kv"].rearrange("(p k) n -> p k n", k=KT)[:, :, c * WC:(c + 1) * WC]
                if kind == "wo":
                    w = a["w_out_a"] if l == 0 else a["w_out_b"]
                    return w[0].rearrange("(k p) n -> p k n", p=P)[:, :, c * WC:(c + 1) * WC]
                if kind == "in":
                    return a["moe_w_in"][l, bass.ds(g, 1), c % EPG].rearrange("o (p k) n -> p (o k n)", k=KT)
                return a["moe_w_down"][l, bass.ds(g, 1), c % EPG].rearrange("o p n -> p (o n)")

            def load_weight(n, g=None):
                kind, l, c = CHUNKS[n]
                if RPREV[n] >= 0:
                    lo_made(sp, RPREV[n])
                to = wraw(n)[:, 0:width(n)]
                if kind == "glu":
                    w = a["w_in_a"][0].rearrange("(p k) n -> p k n", k=KT)
                    to = to.rearrange("p (k h c) -> p k h c", k=KT, h=2)
                    src = w[:, :, 0:2 * CC].rearrange("p k (h c) -> p k h c", h=2)[:, :, :, c * P:(c + 1) * P]
                    sp.dma_start(to[:, :, 0, :], src[:, :, 0, :]).then_inc(w_raw[RSLOT[n]], 8 * 2)
                    sp.dma_start(to[:, :, 1, :], src[:, :, 1, :]).then_inc(w_raw[RSLOT[n]], 8 * 2)
                    return
                src = weight_source(n, g)
                if kind not in ("in", "dn"):
                    to = to.rearrange("p (k n) -> p k n", n=WC)
                sp.dma_start(to, src).then_inc(w_raw[RSLOT[n]], 16)

            def load_x(src):
                for t in range(TT):
                    sp.dma_start(X[:, t, :], src[t * P:(t + 1) * P, :]).then_inc(sem(f"x_in{t}"), 16)

            def moe_weights(l):
                sp.wait_ge(sem("grp_ready"), l + 1)
                g = None
                for s in range(NSTEP + 1):
                    if s < NSTEP:
                        before = g
                        if s % EPG == 0:
                            i = s // EPG
                            g = sp.value_load(grp[0:1, i:i + 1], min_val=0, max_val=G - 1)
                        load_weight(CH["in", l, s], g)
                    if s >= 1:
                        load_weight(CH["dn", l, s - 1], before if s % EPG == 0 and s < NSTEP else g)
                    i = (s - 7) // EPG
                    if s >= 7 and (s - 7) % EPG == 0 and i < NMT - 1:
                        store_y(l, i)

            def store_y(l, i):
                sp.wait_ge(sem("y_out_a"), l * NMT + i + 1)
                sp.wait_ge(sem("y_out_v"), l * NMT + i + 1)
                dst = ybuf[l].rearrange("(s p) n -> p s n", p=P)[:, 2 * i:2 * i + 2, :]
                sp.dma_start(dst, E["ysb"][:, i % 2, :, :]).then_inc(sem(f"y_stored{i % 2}"), 16)

            for t in range(MT):
                sp.dma_start(E["memb"][:, t, :], a["mem"][0, t * P:(t + 1) * P, :]).then_inc(sem("mem_in"), 16)
            load_weight(0)
            load_weight(1)
            load_x(a["x"][0])
            for n in range(2, CH["wo", 0, 2]):
                load_weight(n)
            sp.wait_ge(sem("ln_lo"), CT)
            load_x(a["x"][0])
            load_weight(CH["wo", 0, 2])
            load_weight(CH["wo", 0, 3])
            moe_weights(0)
            n0 = CH["kv", 0, 0]
            load_weight(n0)
            load_weight(n0 + 1)
            store_y(0, NMT - 1)
            for n in range(n0 + 2, CH["wo", 1, 2]):
                load_weight(n)
            sp.wait_ge(sem("sbo_lo"), 2 * SH)
            sp.wait_ge(sem("x_saved"), 16 * TT)
            load_x(xsave)
            load_weight(CH["wo", 1, 2])
            load_weight(CH["wo", 1, 3])
            moe_weights(1)
            store_y(1, NMT - 1)
            for t in range(TT):
                sp.wait_ge(sem("x_sum"), TT + t + 1)
                sp.dma_start(out[0, t * P:(t + 1) * P, :], X[:, t, :]).then_inc(sem("out_stored"), 16)
            sp.wait_ge(sem("out_stored"), 16 * TT)

        @block.gpsimd
        def _(pool):
            step = [0]

            def link(ins):
                step[0] += 1
                ins.then_inc(p_step, 1)
                pool.wait_ge(p_step, step[0])

            at = [0]

            def advance(n):
                while at[0] < len(CHUNKS) and at[0] <= n + 2 and PREV[at[0]] <= n - 1:
                    m = at[0]
                    at[0] += 1
                    w = min(LO_P[m], width(m))
                    if not w:
                        continue
                    pool.wait_ge(w_hi, m + 1)
                    pool.tensor_tensor(wlo(m)[:, 0:w], wraw(m)[:, 0:w], whi(m)[:, 0:w].bitcast(F32),
                                       ALU.subtract).then_inc(w_lo_p, 1)

            link(pool.memset(ident[:], 0.0))
            link(pool.affine_select(out=ident[:], in_=ident[:], compare_op=ALU.not_equal, fill=1.0, base=0,
                                    pattern=[[-1, P]], channel_multiplier=1))
            link(pool.memset(nuinc[:], -1.0))
            link(pool.affine_select(out=nuinc[:], in_=nuinc[:], compare_op=ALU.is_ge, fill=0.0, base=0,
                                    pattern=[[-1, P]], channel_multiplier=1))
            link(pool.memset(lstrict[:], 1.0))
            link(pool.affine_select(out=lstrict[:], in_=lstrict[:], compare_op=ALU.is_gt, fill=0.0, base=0,
                                    pattern=[[1, P]], channel_multiplier=-1))
            link(pool.memset(negm[:], 0.0))
            link(pool.affine_select(out=negm[:], in_=negm[:], compare_op=ALU.is_gt, fill=-BIG, base=0,
                                    pattern=[[1, P]], channel_multiplier=-1))
            link(pool.memset(ones[:], 1.0))
            link(pool.memset(nones[:], -1.0))
            link(pool.memset(eps_t[:], EPS))
            for g in range(4):
                link(pool.memset(desc[:, g:g + 1], float(4 - g)))
            link(pool.iota(iota_i[:], pattern=[[1, P]], base=0, channel_multiplier=0))
            link(pool.tensor_copy(iota[:], iota_i[:]))
            link(pool.iota(iota_i[:, 0:TT], pattern=[[P, TT]], base=0, channel_multiplier=1))
            pool.tensor_copy(tokid[:], iota_i[:, 0:TT]).then_inc(sem("consts"), 1)

            for n in range(0, CH["in", 0, 0]):
                advance(n)

            def moe(l):
                def gather_x(i, sub):
                    if i >= 1:
                        pool.wait_ge(xp_ready, JOB["x", l, i - 1, 2 * sub + 1] + 1)
                    pool.indirect_dma_start(out=A["xg"][:, sub, :], out_offset=None, in_=hn[l],
                                            in_offset=bass.IndirectOffsetOnAxis(ap=idx[:, 2 * i + sub:2 * i + sub + 1], axis=0)
                                            ).then_inc(sem(f"xg_in{sub}"), 16)

                for i in range(2):
                    pool.wait_ge(sem(f"hn_stored{i}"), 16 * (TT // 2) * (l + 1))
                pool.wait_ge(sem("idx_ready"), l + 1)
                gather_x(0, 0)
                gather_x(0, 1)
                gather_x(1, 0)
                for s in range(NSTEP):
                    i, e = divmod(s, EPG)
                    if e == 0 and i + 1 < NMT:
                        gather_x(i + 1, 1)
                    if e == 2 and i + 2 < NMT:
                        gather_x(i + 2, 0)
                    advance(CH["in", l, s])
                    if s >= 1:
                        advance(CH["dn", l, s - 1])
                advance(CH["dn", l, NSTEP - 1])
                for i in range(2):
                    pool.wait_ge(sem(f"y_stored{i}"), 16 * (l + 1) * ((NMT + 1 - i) // 2))
                for t in range(TT):
                    pool.indirect_dma_start(out=A["yg"][:, t, :], out_offset=None, in_=ybuf[l],
                                            in_offset=bass.IndirectOffsetOnAxis(ap=slot_i[:, t:t + 1], axis=0)
                                            ).then_inc(sem(f"yg_in{t}"), 16)

            moe(0)
            for n in range(CH["kv", 0, 0], CH["in", 1, 0]):
                advance(n)
            moe(1)

        @block.scalar
        def _(act):
            step = [0]

            def link(ins):
                step[0] += 1
                ins.then_inc(a_step, 1)
                act.wait_ge(a_step, step[0])

            at = [0]

            def advance(n):
                while at[0] < len(CHUNKS) and at[0] <= n + 2 and PREV[at[0]] <= n - 1:
                    m = at[0]
                    at[0] += 1
                    act.wait_ge(w_raw[RSLOT[m]], raw_count(m))
                    if PREV[m] >= 0:
                        chunk_done(act, PREV[m])
                    w = width(m)
                    gain = weight_gain(m)
                    if gain is None:
                        act.activation(whi(m)[:, 0:w], wraw(m)[:, 0:w], ACT.Copy).then_inc(w_hi, 1)
                    else:
                        act.wait_ge(sem("small_in"), 16 * 15)
                        for k in range(KT):
                            ws = slice(k * WC, (k + 1) * WC)
                            ins = act.activation(whi(m)[:, ws], wraw(m)[:, ws], ACT.Copy, scale=gain[:, k:k + 1])
                        ins.then_inc(w_hi, 1)

            def raw_count(n):
                return sum(32 if CHUNKS[m][0] == "glu" else 16 for m in range(n + 1) if RSLOT[m] == RSLOT[n])

            def load_gain(name):
                vec = {"nmem": a["mem_norm_g"], "nmix0": a["mix_norm_g"][0], "ffn0": a["ffn_norm_g"][0],
                       "ffn1": a["ffn_norm_g"][1]}[name]
                act.dma_start(gb[:], vec.partition_broadcast(P)).then_inc(sem("gain_in"), 16)

            def load_router(l):
                act.dma_start(rw[:, 0], a["router_g_w"][l].rearrange("(p k) g -> p k g", k=KT)).then_inc(sem("router_in"), 16)
                act.dma_start(rw[:, 1:5], a["router_e_w"][l].rearrange("g (p k) e -> p g k e", k=KT)).then_inc(sem("router_in"), 16)
                act.dma_start(rbias[:, 0:4], a["router_g_b"][l].partition_broadcast(P)).then_inc(sem("router_in"), 16)
                act.dma_start(rbias[:, 4:20], a["router_e_b"][l].rearrange("g e -> (g e)").partition_broadcast(P)
                              ).then_inc(sem("router_in"), 16)

            def stats(name, source, tiles, ready):
                for t in range(tiles):
                    ready(t)
                    m = SQ_BASE[name] + t
                    if m >= 1:
                        act.wait_ge(sem("sq_ready"), m)
                    act.activation(junk[:], source(t), ACT.Square, accum_out=ssqx[:, t:t + 1]).then_inc(sem("sq_ready"), 1)

            def out_hi(key, pairs):
                act.wait_ge(xp_ready, JOB[key] + 1)
                for dst, src in pairs:
                    ins = act.activation(dst, src, ACT.Copy)
                ins.then_inc(xp_act, 1)

            def half_view(key):
                return bank(JOB[key] % 2).rearrange("p (k t) -> p k t", k=4)

            def norm_out(name, tiles, next_gain=None):
                for t in range(tiles):
                    for h in range(2):
                        v = half_view((name, t, h))
                        out_hi((name, t, h), [(hi, v[:, k0:k1, :]) for k0, k1, hi, _ in halves(name, t, h)])
                if next_gain:
                    load_gain(next_gain)

            def tile_copy(key, dst):
                act.wait_ge(pj_ready, TILE[key] + 1)
                b = 2 + TILE[key] % 4
                act.activation(dst, PS[:, b, 0:WC], ACT.Copy).then_inc(pj_a, 1)

            def heads_out(name, gain, dst):
                for pr in range(2):
                    for h in range(2):
                        key = (name, pr, h)
                        act.wait_ge(xp_ready, JOB[key] + 1)
                        act.activation(dst(pr, h), bank(JOB[key] % 2), ACT.Copy, scale=gcol[:, gain:gain + 1]
                                       ).then_inc(xp_act, 1)

            def memory_attention(l):
                pb, pt, nb = C[f"pb{l}"], C[f"pt{l}"], 2 - l
                k0 = 6 if l == 0 else 4
                for t in range(TT + 1):
                    if t < TT:
                        act.wait_ge(sem("s_max"), l * TT + t + 1)
                        if t >= nb:
                            act.wait_ge(xp_ready, JOB["p", l, t - nb, 1] + 1)
                        for h in range(MH):
                            at_ = h % 2 * 2 + h // 2
                            ins = act.activation(pb[:, t % nb, h * MEM:(h + 1) * MEM],
                                                 banks(2)[:, at_ * MEM:(at_ + 1) * MEM], ACT.Exp,
                                                 bias=nmx[:, t, at_:at_ + 1], accum_out=psm[:, t, h:h + 1])
                        ins.then_inc(sem("p_ready"), 1)
                        for h in range(2):
                            key = ("p", l, t, h)
                            if t >= nb and h == 0:
                                act.wait_ge(sem("pv_ready"), l * TT + t - nb + 1)
                            out_hi(key, [(pt[:, t % nb, h * 512:(h + 1) * 512], bank(JOB[key] % 2))])
                    if t >= 1:
                        key = ("o", l, t - 1)
                        v = bank(JOB[key] % 2)[:, 0:2 * P].rearrange("p (k t) -> p k t", k=2)
                        tok = slice((t - 1) * P, t * P)
                        dst = B["hth_b"][:, :, tok] if l == 0 else A["hth_a"][:, 4:6, tok]
                        out_hi(key, [(dst, v)])

            def router_and_dispatch(l):
                for t in range(TT):
                    act.wait_ge(h_ready, NT_BASE[f"ffn{l}"] + t + 1)
                    act.dma_start(hn[l][t * P:(t + 1) * P, :], hb[:, (t % 2) * D:(t % 2) * D + D]
                                  ).then_inc(sem(f"hn_stored{t % 2}"), 16)
                    for h in range(2):
                        key = (f"ffn{l}", t, h)
                        if h == 0 and t >= 2:
                            act.wait_ge(sem("lg_ready"), l * TT + t - 1)
                        out_hi(key, [(E["rT"][:, t % 2, 4 * h:4 * h + 4, :], half_view(key))])
                act.wait_ge(sem("dg_ready"), l + 1)
                act.activation(E["rt"][:, 1, 0:32], E["rt"][:, 1, 0:32], ACT.Exp).then_inc(sem("eg_ready"), 1)
                act.wait_ge(sem("dm_ready"), l + 1)
                act.activation(E["rt"][:, 2, 0:8], E["rt"][:, 2, 0:8], ACT.Exp).then_inc(sem("em_ready"), 1)
                if l == 0:
                    load_router(1)

            def moe(l):
                for h in range(4):
                    x_out(l, 0, h)
                for s in range(NSTEP + 1):
                    i, e = divmod(s, EPG)
                    if s < NSTEP and i + 1 < NMT:
                        x_out(l, i + 1, e)
                    if s >= 1:
                        key = ("act", l, s - 1)
                        out_hi(key, [(A["ath"][:, (s - 1) % 2, :], bank(JOB[key] % 2)[:, 0:2 * P])])
                        if s % EPG == 1 and s > EPG:
                            y_out(l, s // EPG - 1)
                    if s < NSTEP:
                        advance(CH["in", l, s])
                        for sub in range(2):
                            act.wait_ge(sem("hid_ready"), 2 * (l * NSTEP + s) + sub + 1)
                            if s >= 2 and sub == 0:
                                act.wait_ge(sem("act_ready"), 2 * (l * NSTEP + s - 1))
                            act.activation(E["sgm"][:, s % 2, sub, :], PS[:, 6 + sub, 0:HID],
                                           ACT.Silu).then_inc(sem("silu_ready"), 1)
                    if s >= 1:
                        advance(CH["dn", l, s - 1])
                y_out(l, NMT - 1)

            def x_out(l, i, h):
                key = ("x", l, i, h)
                sub, half = divmod(h, 2)
                out_hi(key, [(A["xth"][:, i % 2, 4 * half:4 * half + 4, sub * P:(sub + 1) * P], half_view(key))])

            def y_out(l, i):
                act.wait_ge(sem("down_ready"), l * NSTEP + EPG * (i + 1))
                if i >= 2 or l:
                    wait_stored(l, i)
                act.activation(E["ysb"][:, i % 2, 0, :], banks(2), ACT.Copy).then_inc(sem("y_out_a"), 1)

            def wait_stored(l, i):
                if i >= 2:
                    act.wait_ge(sem(f"y_stored{i % 2}"), 16 * (l * ((NMT + 1 - i % 2) // 2) + i // 2))

            load_gain("nmem")
            act.dma_start(E["cwr"][0:CW, :], a["conv_w"][0]).then_inc(sem("small_in"), 16)
            act.dma_start(E["cwr"][CW:CW + 1, :], a["conv_ln_g"]).then_inc(sem("small_in"), 16)
            act.dma_start(E["cwr"][CW + 1:CW + 2, :], a["conv_ln_b"]).then_inc(sem("small_in"), 16)
            for l in range(2):
                for h in range(2):
                    act.dma_start(gr[l:l + 1, h * MHD:(h + 1) * MHD], a["mem_q_norm_g"][l:l + 1, :]).then_inc(sem("small_in"), 16)
                    act.dma_start(gr[2 + l:3 + l, h * MHD:(h + 1) * MHD], a["mem_k_norm_g"][l:l + 1, :]).then_inc(sem("small_in"), 16)
            act.dma_start(gr[4:5, :], a["sb_q_norm_g"]).then_inc(sem("small_in"), 16)
            act.dma_start(gr[5:6, :], a["sb_k_norm_g"].rearrange("(o n) -> o n", o=1)).then_inc(sem("small_in"), 16)
            act.dma_start(gkv[:], a["kv_norm_g"].rearrange("(p k) -> p k", k=KT)).then_inc(sem("small_in"), 16)
            act.dma_start(gmix1[:], a["mix_norm_g"][1].rearrange("(p k) -> p k", k=KT)).then_inc(sem("small_in"), 16)
            load_router(0)

            stats("nmem", lambda t: E["memb"][:, t, :], MT, lambda t: act.wait_ge(sem("mem_in"), 16 * MT))
            act.wait_ge(xp_ready, JOB[("cw",)] + 1)
            act.activation(cw[:].rearrange("p c w -> p (c w)"), PS[:, 0, 0:CT * (CW + 2)], ACT.Copy)
            act.activation(gcol[:, 0:6], PS[:, 0, 256:262], ACT.Copy).then_inc(xp_act, 1)
            norm_out("nmem", MT, "nmix0")
            for n in range(4):
                l, c = divmod(n, 2)
                advance(n)
                for t in range(MT):
                    tile_copy(("mem", l, c, t), E["mkraw"][:, l, t, :] if c == 0 else mv[:, l, t, :])
            act.wait_ge(sem("gcol_ready"), 1)
            for l in range(2):
                act.wait_ge(xp_ready, JOB["mk", l] + 1)
                act.activation(mkT[:, l].rearrange("p a m -> p (a m)"), bank(JOB["mk", l] % 2), ACT.Copy,
                               scale=gcol[:, 2 + l:3 + l]).then_inc(xp_act, 1)

            stats("nmix0", lambda t: X[:, t, :], TT, lambda t: act.wait_ge(sem(f"x_in{t}"), 16))
            norm_out("nmix0", TT, "ffn0")
            for c in range(CT):
                if c == GLU_FIRST:
                    advance(CH["qm", 0, 0])
                    for t in range(TT):
                        tile_copy(("qm", 0, 0, t), hb[:, t * WC:(t + 1) * WC])
                advance(CH["glu", 0, c])
                for h in range(2):
                    s = 2 * c + h
                    act.wait_ge(sem("glu_ready"), s + 1)
                    if s >= 2:
                        act.wait_ge(sem("cin_ready"), s - 1)
                    act.activation(C["sg"][:, s % 2, :], bank(3 + 2 * (s % 2)), ACT.Sigmoid).then_inc(sem("sig_ready"), 1)
            heads_out("hm0", 0, lambda pr, h: C["qmT0"][:, pr, h * 512:(h + 1) * 512])
            memory_attention(0)
            advance(CH["wo", 0, 0] - 1)
            for c in range(CT):
                act.wait_ge(sem("xc_ready"), c + 1)
                if c >= 2:
                    act.wait_ge(sem("var_used"), c - 1)
                act.activation(C["pb0"][:, c % 2, :], E["cv"][:, c, :], ACT.Square).then_inc(sem("xsq_ready"), 1)
            act.wait_ge(sem("var_used"), CT)
            act.activation(C["pt0"][:, 0, :], banks(2), ACT.Sqrt, scale=1.0 / CC, bias=eps_t[:]).then_inc(sem("std_ready"), 1)
            for c in range(CT):
                act.wait_ge(sem("y0_ready"), c + 1)
                if c >= 2:
                    act.wait_ge(sem("ln_lo"), c - 1)
                link(act.activation(C["pb0"][:, c % 2, :], E["cv"][:, c, :], ACT.Silu, scale=cw[:, c, CW:CW + 1],
                                    bias=cw[:, c, CW + 1:CW + 2]))
                act.activation(A["hth_a"][:, c, :], C["pb0"][:, c % 2, :], ACT.Copy).then_inc(sem("ln_hi"), 1)
            for c in range(4):
                advance(CH["wo", 0, c])

            def ffn(l):
                stats(f"ffn{l}", lambda t: X[:, t, :], TT, lambda t: tile_out(act, ("wo", l, 3, t)))
                router_and_dispatch(l)
                moe(l)

            ffn(0)
            def saved(t):
                act.wait_ge(sem("x_sum"), t + 1)
                act.dma_start(xsave[t * P:(t + 1) * P, :], X[:, t, :]).then_inc(sem("x_saved"), 16)

            stats("nkv", lambda t: X[:, t, :], TT, saved)
            norm_out("nkv", TT, "ffn1")
            for j in range(2):
                for c in (j, 2 + j):
                    advance(CH["kv", 0, c])
                    for t in range(TT):
                        tile_copy(("kv", 0, c, t), hb[:, t * WC:(t + 1) * WC] if c < 2 else
                                  E["V"][:, t, j * WC:(j + 1) * WC])
                heads_out(f"hk{j}", 5, lambda pr, h: E["kT"][:, 2 * j + pr, h * 512:(h + 1) * 512])
            act.wait_ge(sem("x_saved"), 16 * TT)
            def raw_out(kind, j, to):
                advance(CH[kind, 1, j])
                for t in range(TT):
                    tile_copy((kind, 1, j, t), to[:, t * WC:(t + 1) * WC])

            def queries_out(j):
                heads_out(f"hq{j}", 4, lambda pr, h: C["qT"][:, 2 * j + pr, h * 512:(h + 1) * 512])

            raw_out("qm", 0, hb)
            raw_out("qs", 0, C["hb2"])
            heads_out("hm1", 1, lambda pr, h: C["qmT1"][:, pr, h * 512:(h + 1) * 512])
            raw_out("qs", 1, hb)
            queries_out(0)
            memory_attention(1)
            queries_out(1)
            advance(CH["wo", 1, 0] - 1)

            def head_out(head):
                act.wait_ge(sem("av_ready"), (head + 1) * NSB)
                for h in range(2):
                    act.activation(A["hth_a"][:, head, h * 512:(h + 1) * 512], bank(4 + 2 * (head % 2) + h), ACT.Copy
                                   ).then_inc(sem("sbo_hi"), 1)

            act.add_instruction(mybir.InstLoadActFuncSet(act_func_set_id=LN_EXP_SET, name=f"I-{nc.next_id()}", engine=act.engine,
                                                         ins=[], outs=[]))
            for head in range(SH):
                for i in range(NSB + 1):
                    n = head * NSB + i
                    if i < NSB:
                        b, q0, w, diag = SB_STEPS[i]
                        lt = C["lt"][:, n % 3, 0:w]
                        act.wait_ge(sem("z_ready"), n + 1)
                        if n >= 3:
                            act.wait_ge(sem("sp_ready"), n - 2)
                        link(act.activation(lt, PS[:, n % ZB, 0:w], ACT.Abs))
                        link(act.activation(lt, lt, ACT.Exp, scale=-1.0))
                        act.activation(lt, lt, ACT.Ln, bias=1.0).then_inc(sem("l_ready"), 1)
                    if i >= 1:
                        m = n - 1
                        b, q0, w, diag = SB_STEPS[i - 1]
                        act.wait_ge(sem("r_ready"), m + 1)
                        if m >= 2:
                            act.wait_ge(sem("av_ready"), m - 1)
                        act.activation(B["wgt"][:, m % 2, 0:w], PS[:, m % ZB, 0:w], ACT.Exp).then_inc(sem("wgt_ready"), 1)
                    if i == 3 and head:
                        head_out(head - 1)
            head_out(SH - 1)
            for c in range(4):
                advance(CH["wo", 1, c])
            ffn(1)

        @block.vector
        def _(dve):
            step = [0]

            def link(ins):
                step[0] += 1
                ins.then_inc(v_step, 1)
                dve.wait_ge(v_step, step[0])

            at = [0]

            def advance(n):
                while at[0] < len(CHUNKS) and at[0] <= n + 2 and PREV[at[0]] <= n - 1:
                    m = at[0]
                    at[0] += 1
                    if LO_P[m] >= 2048:
                        continue
                    dve.wait_ge(w_hi, m + 1)
                    gain = weight_gain(m)
                    if gain is not None:
                        dve.wait_ge(sem("small_in"), 16 * 15)
                        for k in range(KT):
                            ws = slice(k * WC, (k + 1) * WC)
                            ins = dve.scalar_tensor_tensor(out=wlo(m)[:, ws], in0=wraw(m)[:, ws], scalar=gain[:, k:k + 1],
                                                           in1=whi(m)[:, ws].bitcast(F32), op0=ALU.mult, op1=ALU.subtract)
                        ins.then_inc(w_lo_v, 1)
                        continue
                    w = slice(LO_P[m], width(m))
                    dve.tensor_tensor(wlo(m)[:, w], wraw(m)[:, w], whi(m)[:, w].bitcast(F32),
                                      ALU.subtract).then_inc(w_lo_v, 1)

            def rsqrt(to, squares, n, count):
                x, y, t = nx[:, 0:n], ny[:, 0:n], nt_[:, 0:n]
                link(dve.tensor_scalar(x, squares[:, 0:n], 1.0 / count, EPS, ALU.mult, ALU.add))
                link(dve.tensor_single_scalar(t.bitcast(I32), x.bitcast(I32), 1, ALU.arith_shift_right))
                link(dve.tensor_scalar(y.bitcast(I32), t.bitcast(I32), -1.0, 1597463007.0, ALU.mult, ALU.add))
                for k in range(3):
                    link(dve.tensor_tensor(t, y, y, ALU.mult))
                    link(dve.scalar_tensor_tensor(out=t, in0=t, scalar=-0.5, in1=x, op0=ALU.mult, op1=ALU.mult))
                    link(dve.scalar_tensor_tensor(out=y if k < 2 else to[:, 0:n], in0=t, scalar=1.5, in1=y,
                                                  op0=ALU.add, op1=ALU.mult))

            def out_lo(key, trios):
                dve.wait_ge(xp_act, JOB[key] + 1)
                for dst, src, hi in trios:
                    ins = dve.tensor_tensor(dst, src, hi.bitcast(F32), ALU.subtract)
                ins.then_inc(xp_dve, 1)

            def half_view(key):
                return bank(JOB[key] % 2).rearrange("p (k t) -> p k t", k=4)

            def norm(name, source, tiles, lo=True, gain=True):
                dve.wait_ge(sem("sq_ready"), SQ_BASE[name] + tiles)
                rsqrt(rsx, ssqx, tiles, D)
                if gain:
                    dve.wait_ge(sem("gain_in"), 16 * GB[name])
                if name in HB_BEFORE:
                    dve.wait_ge(xp_ready, JOB[HB_BEFORE[name]] + 1)

                def h_tile(t):
                    if t >= 2:
                        dve.wait_ge(xp_ready, JOB[name, t - 2, 1] + 1)
                        if not lo:
                            dve.wait_ge(sem(f"hn_stored{t % 2}"), 16 * (int(name[3]) * (TT // 2) + t // 2))
                    h = hb[:, (t % 2) * D:(t % 2) * D + D]
                    if gain:
                        dve.scalar_tensor_tensor(out=h, in0=source(t), scalar=rsx[:, t:t + 1], in1=gb[:], op0=ALU.mult,
                                                 op1=ALU.mult).then_inc(h_ready, 1)
                    else:
                        dve.tensor_scalar(h, source(t), rsx[:, t:t + 1], None, ALU.mult).then_inc(h_ready, 1)

                for t in range(tiles + 1):
                    if t < tiles:
                        h_tile(t)
                    if t >= 1 and lo:
                        for h in range(2):
                            v = half_view((name, t - 1, h))
                            out_lo((name, t - 1, h), [(lo_, v[:, k0:k1, :], hi) for k0, k1, hi, lo_ in halves(name, t - 1, h)])

            def head_norm(name):
                kind, l, c = HN_CHUNK[name]
                nh, hd = (MH, MHD) if kind == "qm" else (2, SHD)
                tile_out(dve, (kind, l, c, TT - 1))
                v = raw_heads(name)[:].rearrange("p (a d) -> p a d", d=hd)
                for i in range(TT * nh):
                    ins = dve.tensor_tensor_reduce(out=junk[:, (i * hd) % D:(i * hd) % D + hd], in0=v[:, i, :], in1=v[:, i, :],
                                                   scale=1.0, scalar=0.0, op0=ALU.mult, op1=ALU.add, accum_out=ssq[:, i:i + 1])
                    if i in (TT * nh // 2 - 1, TT * nh - 1):
                        link(ins)
                rsqrt(rs, ssq, TT * nh, hd)
                dve.tensor_tensor(v, v, rs[:, 0:TT * nh].unsqueeze(2).to_broadcast([P, TT * nh, hd]), ALU.mult
                                  ).then_inc(sem("hn_ready"), 1)

            def attention_steps(l):
                on = C["on0"] if l == 0 else B["on1"]

                def maxima(t):
                    dve.wait_ge(sem("s_ready"), l * TT + t + 1)
                    link(dve.tensor_reduce(mx[:, t, :], banks(2).rearrange("p (h m) -> p h m", h=MH), AX, ALU.max))
                    dve.tensor_scalar(nmx[:, t, :], mx[:, t, :], -1.0, None, ALU.mult).then_inc(sem("s_max"), 1)

                def outputs(t):
                    dve.wait_ge(sem("p_ready"), l * TT + t + 1)
                    link(dve.reciprocal(pri[:, t, :], psm[:, t, :]))
                    dve.wait_ge(sem("pv_ready"), l * TT + t + 1)
                    if t >= 2:
                        dve.wait_ge(xp_ready, JOB["o", l, t - 2] + 1)
                    dve.tensor_tensor(on[:, t % 2, :].rearrange("p (h d) -> p h d", h=MH),
                                      PS[:, 4 + t % 2, 0:MW].rearrange("p (h d) -> p h d", h=MH),
                                      pri[:, t, :].unsqueeze(2).to_broadcast([P, MH, MHD]), ALU.mult
                                      ).then_inc(sem("on_ready"), 1)

                def lows(t):
                    key = ("o", l, t)
                    v = bank(JOB[key] % 2)[:, 0:2 * P].rearrange("p (k t) -> p k t", k=2)
                    tok = slice(t * P, (t + 1) * P)
                    hi, lo = (B["hth_b"][:, :, tok], B["htl_b"][:, :, tok]) if l == 0 else \
                        (A["hth_a"][:, 4:6, tok], A["htl_a"][:, 4:6, tok])
                    out_lo(key, [(lo, v, hi)])

                steps = [lambda: maxima(0)]
                for t in range(TT):
                    if t + 1 < TT:
                        steps.append(lambda t=t: maxima(t + 1))
                    if t >= 1:
                        steps.append(lambda t=t: lows(t - 1))
                    steps.append(lambda t=t: outputs(t))
                return steps + [lambda: lows(TT - 1)]

            def dispatch(l):
                rt = E["rt"]

                def r(n, k, shape=None):
                    v = rt[:, n, 0:k]
                    return v if shape is None else v.rearrange(shape[0], **shape[1])

                dve.wait_ge(sem("lg_ready"), TT * (l + 1))
                dve.wait_ge(sem("router_in"), 64 * (l + 1))
                lg = rt[:, 0, 0:160].rearrange("p (t c) -> p t c", t=TT)
                link(dve.tensor_tensor(lg, PS[:, 2, 0:160].rearrange("p (t c) -> p t c", t=TT),
                                       rbias[:].unsqueeze(1).to_broadcast([P, TT, 20]), ALU.add))
                glog = lg[:, :, 0:4]
                dg = rt[:, 1, 0:32].rearrange("p (t g) -> p t g", g=4)
                gmax, m1, m2, mm = (rt[:, 3, 8 * k:8 * k + 8] for k in range(4))
                oh = rt[:, 4, 0:32].rearrange("p (t g) -> p t g", g=4)
                o1 = rt[:, 4, 32:64].rearrange("p (t g) -> p t g", g=4)
                o2 = rt[:, 4, 64:96].rearrange("p (t g) -> p t g", g=4)
                pr = rt[:, 4, 96:128].rearrange("p (t g) -> p t g", g=4)
                sel = rt[:, 5, 0:32].rearrange("p (t g) -> p t g", g=4)
                sel2 = rt[:, 5, 32:64].rearrange("p (t g) -> p t g", g=4)
                eg = rt[:, 5, 64:96].rearrange("p (t g) -> p t g", g=4)
                eg2 = rt[:, 5, 96:128].rearrange("p (t g) -> p t g", g=4)
                gg = rt[:, 3, 32:40]
                w1, w2, pm = rt[:, 3, 40:48], rt[:, 3, 48:56], rt[:, 3, 56:64]

                def over(v, n=4):
                    return v.unsqueeze(2).to_broadcast([P, TT, n])

                def first_max(values, top, onehot):
                    link(dve.tensor_reduce(top, values, AX, ALU.max))
                    link(dve.tensor_tensor(pr, values, over(top), ALU.is_equal))
                    link(dve.tensor_tensor(pr, pr, desc[:].unsqueeze(1).to_broadcast([P, TT, 4]), ALU.mult))
                    link(dve.tensor_reduce(pm, pr, AX, ALU.max))
                    link(dve.tensor_tensor(onehot, pr, over(pm), ALU.is_equal))

                first_max(glog, gmax, oh)
                dve.tensor_tensor(dg, glog, over(gmax), ALU.subtract).then_inc(sem("dg_ready"), 1)
                dve.tensor_copy(rt[:, 6, 0:32].rearrange("p (t g) -> p t g", g=4), oh).then_inc(sem("oh_ready"), 1)
                se = rt[:, 7, 0:128].rearrange("p (t g e) -> p t g e", t=TT, g=4)
                link(dve.tensor_tensor(se, lg[:, :, 4:20].rearrange("p t (g e) -> p t g e", g=4),
                                       oh.unsqueeze(3).to_broadcast([P, TT, 4, 4]), ALU.mult))
                link(dve.tensor_reduce(sel, se.rearrange("p t g e -> p t e g"), AX, ALU.add))
                first_max(sel, m1, o1)
                link(dve.scalar_tensor_tensor(out=sel2, in0=o1, scalar=-BIG, in1=sel, op0=ALU.mult, op1=ALU.add))
                first_max(sel2, m2, o2)
                dve.tensor_tensor(rt[:, 2, 0:8], m2, m1, ALU.subtract).then_inc(sem("dm_ready"), 1)
                dve.wait_ge(sem("eg_ready"), l + 1)
                link(dve.tensor_reduce(gg, dg, AX, ALU.add))
                dve.wait_ge(sem("em_ready"), l + 1)
                link(dve.tensor_scalar(mm, rt[:, 2, 0:8], 1.0, None, ALU.add))
                link(dve.tensor_tensor(mm, mm, gg, ALU.mult))
                link(dve.reciprocal(w1, mm))
                link(dve.tensor_tensor(w2, w1, rt[:, 2, 0:8], ALU.mult))
                link(dve.tensor_tensor(eg, o1, over(w1), ALU.mult))
                link(dve.tensor_tensor(eg2, o2, over(w2), ALU.mult))
                link(dve.tensor_tensor(eg, eg, eg2, ALU.add))
                dve.wait_ge(sem("cnt_ready"), l + 1)
                pc = rt[:, 6, 32:96]
                link(dve.tensor_copy(pc, PS[:, 3, 0:64]))
                pre = pc[:, 0:32].rearrange("p (t g) -> p t g", g=4)
                cnt = pc[:, 32:64].rearrange("p (t g) -> p t g", g=4)
                tb = rt[:, 6, 96:132].rearrange("p (t g) -> p t g", g=4)
                link(dve.memset(tb[:, 0, :], 0.0))
                for t in range(TT):
                    link(dve.tensor_tensor(tb[:, t + 1, :], tb[:, t, :], cnt[:, t, :], ALU.add))
                total, nt, base = tb[:, TT, :], rt[:, 6, 132:136], rt[:, 6, 136:140]
                end = rt[:, 6, 140:144]
                link(dve.tensor_scalar(nt, total, 0.0, None, ALU.is_gt))
                for m in range(1, T // MTILE):
                    link(dve.scalar_tensor_tensor(out=nt, in0=total, scalar=float(m * MTILE), in1=nt,
                                                  op0=ALU.is_gt, op1=ALU.add))
                link(dve.tensor_copy(end, nt))
                for g in range(1, G):
                    link(dve.tensor_tensor(end[:, g:g + 1], end[:, g - 1:g], nt[:, g:g + 1], ALU.add))
                link(dve.tensor_tensor(base, end, nt, ALU.subtract))
                link(dve.tensor_scalar(base, base, float(MTILE), None, ALU.mult))
                cmp = rt[:, 7, 0:28].rearrange("p (i g) -> p i g", g=4)
                link(dve.tensor_tensor(cmp, end.unsqueeze(1).to_broadcast([P, NMT, 4]),
                                       iota[:, 0:NMT].unsqueeze(2).to_broadcast([P, NMT, 4]), ALU.is_le))
                gi = rt[:, 7, 28:28 + NMT]
                link(dve.tensor_reduce(gi, cmp, AX, ALU.add))
                dve.tensor_scalar(grp[:, 0:NMT], gi, float(G - 1), None, ALU.min).then_inc(sem("grp_ready"), 1)
                link(dve.tensor_tensor(pre, pre, tb[:, 0:TT, :], ALU.add))
                link(dve.tensor_tensor(pre, pre, base.unsqueeze(1).to_broadcast([P, TT, 4]), ALU.add))
                link(dve.tensor_tensor(pre, pre, oh, ALU.mult))
                link(dve.tensor_reduce(mm, pre, AX, ALU.add))
                link(dve.tensor_copy(slot_i[:], mm))
                sa, sb_ = rt[:, 7, 40:48], rt[:, 7, 48:56]
                saf, sbf = rt[:, 7, 56:64], rt[:, 7, 64:72]
                link(dve.tensor_single_scalar(sa.bitcast(I32), slot_i[:], 7, ALU.arith_shift_right))
                link(dve.tensor_single_scalar(sb_.bitcast(I32), slot_i[:], P - 1, ALU.bitwise_and))
                link(dve.tensor_copy(saf, sa.bitcast(I32)))
                link(dve.tensor_copy(sbf, sb_.bitcast(I32)))
                vals = rt[:, 2, 16:56].rearrange("p (t v) -> p t v", v=5)
                link(dve.tensor_copy(vals[:, :, 0], tokid[:]))
                link(dve.tensor_copy(vals[:, :, 1:5], eg))
                aoh = rt[:, 0, 0:TT * NSUB].rearrange("p (t a) -> p t a", t=TT)
                link(dve.tensor_tensor(aoh, over(saf, NSUB), iota[:, 0:NSUB].unsqueeze(1).to_broadcast([P, TT, NSUB]),
                                       ALU.is_equal))
                for t in range(TT):
                    dve.tensor_scalar(E["boh"][:, t, :], iota[:], sbf[:, t:t + 1], None, ALU.is_equal)
                dve.tensor_tensor(E["av"][:], aoh.unsqueeze(3).to_broadcast([P, TT, NSUB, 5]),
                                  vals.unsqueeze(2).to_broadcast([P, TT, NSUB, 5]), ALU.mult).then_inc(sem("av_in"), 1)
                dve.wait_ge(sem("slots_ready"), l + 1)
                v = PS[:, 4, 0:NSUB * 5].rearrange("p (a v) -> p a v", v=5)
                link(dve.tensor_copy(gates[:], v[:, :, 1:5]))
                dve.tensor_copy(idx[:], v[:, :, 0]).then_inc(sem("idx_ready"), 1)

            def moe(l):
                def x_low(i, h):
                    key = ("x", l, i, h)
                    sub, half = divmod(h, 2)
                    at_ = (slice(None), i % 2, slice(4 * half, 4 * half + 4), slice(sub * P, (sub + 1) * P))
                    out_lo(key, [(A["xtl"][at_], half_view(key), A["xth"][at_])])

                def y_out(i):
                    dve.wait_ge(sem("down_ready"), l * NSTEP + EPG * (i + 1))
                    if i >= 2:
                        dve.wait_ge(sem(f"y_stored{i % 2}"), 16 * (l * ((NMT + 1 - i % 2) // 2) + i // 2))
                    dve.tensor_copy(E["ysb"][:, i % 2, 1, :], banks(4)).then_inc(sem("y_out_v"), 1)

                for h in range(4):
                    x_low(0, h)
                for s in range(NSTEP + 1):
                    i, e = divmod(s, EPG)
                    if s < NSTEP and i + 1 < NMT:
                        x_low(i + 1, e)
                    if s >= 1:
                        key = ("act", l, s - 1)
                        out_lo(key, [(A["atl"][:, (s - 1) % 2, :], bank(JOB[key] % 2)[:, 0:2 * P], A["ath"][:, (s - 1) % 2, :])])
                        if s % EPG == 1 and s > EPG:
                            y_out(s // EPG - 1)
                    if s < NSTEP:
                        advance(CH["in", l, s])
                        for sub in range(2):
                            dve.wait_ge(sem("silu_ready"), 2 * (l * NSTEP + s) + sub + 1)
                            if s >= 2 and sub == 0:
                                dve.wait_ge(xp_ready, JOB["act", l, s - 2] + 1)
                            u = PS[:, 6 + sub, HID:2 * HID]
                            dve.scalar_tensor_tensor(out=E["actm"][:, s % 2, sub, :], in0=E["sgm"][:, s % 2, sub, :],
                                                     scalar=gates[:, 2 * i + sub, e:e + 1], in1=u, op0=ALU.mult,
                                                     op1=ALU.mult).then_inc(sem("act_ready"), 1)
                    if s >= 1:
                        advance(CH["dn", l, s - 1])
                y_out(NMT - 1)
                for t in range(TT):
                    dve.wait_ge(sem(f"yg_in{t}"), 16 * (l + 1))
                    dve.tensor_tensor(X[:, t, :], X[:, t, :], A["yg"][:, t, :], ALU.add).then_inc(sem("x_sum"), 1)

            def residual(l):
                for c in range(4):
                    advance(CH["wo", l, c])
                    for t in range(TT):
                        key = ("wo", l, c, t)
                        dve.wait_ge(pj_ready, TILE[key] + 1)
                        if c == 0:
                            dve.wait_ge(sem(f"x_in{t}"), 32 + 16 * l)
                        xs = X[:, t, c * WC:(c + 1) * WC]
                        dve.tensor_tensor(xs, xs, PS[:, 2 + TILE[key] % 4, 0:WC], ALU.add).then_inc(pj_v, 1)

            norm("nmem", lambda t: E["memb"][:, t, :], MT)
            dve.wait_ge(xp_act, 1)
            link(dve.tensor_scalar(gcol[:, 0:2], gcol[:, 0:2], float(MHD) ** -0.5, None, ALU.mult))
            dve.tensor_scalar(gcol[:, 4:5], gcol[:, 4:5], float(SHD) ** -0.5, None, ALU.mult).then_inc(sem("gcol_ready"), 1)
            for l in range(2):
                tile_out(dve, ("mem", l, 0, MT - 1))
                v = E["mkraw"][:, l].rearrange("p t (h d) -> p (t h) d", h=MH)
                for i in range(MT * MH):
                    ins = dve.tensor_tensor_reduce(out=junk[:, i * MHD:(i + 1) * MHD], in0=v[:, i, :], in1=v[:, i, :],
                                                   scale=1.0, scalar=0.0, op0=ALU.mult, op1=ALU.add, accum_out=ssq[:, i:i + 1])
                link(ins)
                rsqrt(rs, ssq, MT * MH, MHD)
                dve.tensor_tensor(v, v, rs[:, 0:MT * MH].unsqueeze(2).to_broadcast([P, MT * MH, MHD]), ALU.mult
                                  ).then_inc(sem("mk_ready"), 1)
                dve.wait_ge(sem("mk_ready"), l + 1)

            norm("nmix0", lambda t: X[:, t, :], TT)
            cin, cv = E["cin"], E["cv"]
            dve.wait_ge(xp_act, JOB["mk", 1] + 1)
            link(dve.memset(cin[:, :, 0:CW - 1], 0.0))
            extra = []

            def glu(c):
                for h in range(2):
                    s = 2 * c + h
                    dve.wait_ge(sem("sig_ready"), s + 1)
                    dve.tensor_tensor(cin[:, c % 2, CW - 1 + h * 512:CW - 1 + (h + 1) * 512], bank(2 + 2 * (s % 2)),
                                      C["sg"][:, s % 2, :], ALU.mult).then_inc(sem("cin_ready"), 1)

            glu(0)
            for c in range(CT):
                if c + 1 < CT:
                    glu(c + 1)
                dve.wait_ge(sem("cin_ready"), 2 * c + 2)
                for j in range(CW):
                    src, tap = cin[:, c % 2, j:j + T], cw[:, c, j:j + 1]
                    if j == 0:
                        ins = dve.tensor_scalar(cv[:, c, :], src, tap, None, ALU.mult)
                    else:
                        ins = dve.scalar_tensor_tensor(out=cv[:, c, :], in0=src, scalar=tap, in1=cv[:, c, :],
                                                       op0=ALU.mult, op1=ALU.add)
                    if j < CW - 1:
                        link(ins)
                    else:
                        ins.then_inc(sem("conv_ready"), 1)
                        dve.wait_ge(sem("conv_ready"), c + 1)
                    if c >= GLU_FIRST and extra and j % 2 == 1:
                        extra.pop(0)()
                if c == GLU_FIRST - 1:
                    extra = [lambda: head_norm("hm0")] + attention_steps(0)
            for f in extra:
                f()
            dve.wait_ge(sem("mean_ready"), 1)
            for c in range(CT):
                dve.scalar_tensor_tensor(out=cv[:, c, :], in0=banks(6), scalar=-1.0 / CC, in1=cv[:, c, :], op0=ALU.mult,
                                         op1=ALU.add).then_inc(sem("xc_ready"), 1)
            dve.wait_ge(sem("std_ready"), 1)
            link(dve.reciprocal(C["pt0"][:, 1, :], C["pt0"][:, 0, :]))
            for c in range(CT + 1):
                if c < CT:
                    dve.tensor_tensor(cv[:, c, :], cv[:, c, :], C["pt0"][:, 1, :], ALU.mult).then_inc(sem("y0_ready"), 1)
                if c >= 1:
                    dve.wait_ge(sem("ln_hi"), c)
                    dve.tensor_tensor(A["htl_a"][:, c - 1, :], C["pb0"][:, (c - 1) % 2, :], A["hth_a"][:, c - 1, :].bitcast(F32),
                                      ALU.subtract).then_inc(sem("ln_lo"), 1)
            residual(0)

            def ffn(l):
                norm(f"ffn{l}", lambda t: X[:, t, :], TT, lo=False)
                dispatch(l)
                moe(l)

            ffn(0)
            norm("nkv", lambda t: X[:, t, :], TT, gain=False)
            advance(CH["kv", 0, 2])
            head_norm("hk0")
            advance(CH["kv", 0, 3])
            head_norm("hk1")
            advance(CH["qs", 1, 0])
            head_norm("hm1")
            head_norm("hq0")
            for n, f in enumerate(attention_steps(1)):
                f()
                if n == 7:
                    head_norm("hq1")
            lfsum = B["lfsum"]

            def head_lo(head):
                for h in range(2):
                    dve.wait_ge(sem("sbo_hi"), 2 * head + h + 1)
                    q = slice(h * 512, (h + 1) * 512)
                    dve.tensor_tensor(A["htl_a"][:, head, q], bank(4 + 2 * (head % 2) + h), A["hth_a"][:, head, q].bitcast(F32),
                                      ALU.subtract).then_inc(sem("sbo_lo"), 1)

            for head in range(SH):
                for i, (b, q0, w, diag) in enumerate(SB_STEPS):
                    n = head * NSB + i
                    s = C["sp"][:, n % 3, 0:w]
                    dve.wait_ge(sem("l_ready"), n + 1)
                    if n >= 3:
                        dve.wait_ge(sem("r_ready"), n - 2)
                    dve.scalar_tensor_tensor(out=s, in0=PS[:, n % ZB, 0:w], scalar=0.0, in1=C["lt"][:, n % 3, 0:w],
                                             op0=ALU.max, op1=ALU.add).then_inc(sem("sp_ready"), 1)
                    dve.wait_ge(sem("sp_ready"), n + 1)
                    if i == 3 and head:
                        head_lo(head - 1)
                    if b == 0:
                        continue
                    new, old = lfsum[:, b % 2, :], lfsum[:, (b + 1) % 2, :]
                    last = [m for m in range(n) if SB_STEPS[m % NSB][0] % 2 != b % 2]
                    if last:
                        dve.wait_ge(sem("r_ready"), last[-1] + 1)
                    d = P if diag else 0
                    if diag:
                        ins = dve.tensor_copy(new[:, q0:q0 + P], s[:, 0:P])
                    if w > d:
                        ins = dve.tensor_tensor(new[:, q0 + d:q0 + w], old[:, q0 + d:q0 + w], s[:, d:w], ALU.add)
                    ins.then_inc(sem("sum_ready"), 1)
                    dve.wait_ge(sem("sum_ready"), SUMS(n))
            head_lo(SH - 1)
            residual(1)
            ffn(1)

        @block.tensor
        def _(pe):
            def job(key):
                j = JOB[key]
                if j >= 2:
                    pe.wait_ge(xp_act, j - 1)
                    if JOB_LO[j - 2]:
                        pe.wait_ge(xp_dve, JOB_LO[j - 2])
                return j % 2

            def norm_jobs(name, tiles, after=None):
                for t in range(tiles):
                    pe.wait_ge(h_ready, NT_BASE[name] + t + 1)
                    for h in range(2):
                        b = job((name, t, h))
                        for k in range(4):
                            at_ = (t % 2) * D + 4 * h + k
                            ins = pe.transpose(PS[:, b, k * P:(k + 1) * P], hb[:, at_:at_ + KT * (P - 1) + 1:KT], ident[:])
                        ins.then_inc(xp_ready, 1)
                    if after:
                        after(t)

            def chunk(n):
                pe.wait_ge(w_hi, n + 1)
                lo_made(pe, n)

            def project(kind, l, c, tiles, nk, hi, lo):
                n = CH[kind, l, c]
                chunk(n)
                for t in range(tiles):
                    j = TILE[kind, l, c, t]
                    if j >= 4:
                        tile_out(pe, TILES[j - 4][0])
                    tok = slice(t * P, (t + 1) * P)
                    o = PS[:, 2 + j % 4, 0:WC]
                    for k in range(nk):
                        ws = slice(k * WC, (k + 1) * WC)
                        pe.matmul(o, hi(k)[:, tok], whi(n)[:, ws], start=k == 0, stop=False)
                        pe.matmul(o, hi(k)[:, tok], wlo(n)[:, ws], start=False, stop=False)
                        ins = pe.matmul(o, lo(k)[:, tok], whi(n)[:, ws], start=False, stop=k == nk - 1)
                    ins.then_inc(pj_ready, 1)

            def head_jobs(name):
                kind, l, c = HN_CHUNK[name]
                pe.wait_ge(sem("hn_ready"), HN[name] + 1)
                raw = raw_heads(name)
                for pr in range(2):
                    for h in range(2):
                        b = job((name, pr, h))
                        for q in range(4):
                            t = 4 * h + q
                            ins = pe.transpose(PS[:, b, q * P:(q + 1) * P], raw[:, t * WC + pr * P:t * WC + (pr + 1) * P], ident[:])
                        ins.then_inc(xp_ready, 1)

            def memory_attention(l):
                qmT, pb, pt, nb = C[f"qmT{l}"], C[f"pb{l}"], C[f"pt{l}"], 2 - l
                on = C["on0"] if l == 0 else B["on1"]

                def scores(t):
                    if t >= 1:
                        pe.wait_ge(sem("p_ready"), l * TT + t)
                    for h in range(MH):
                        rows = slice(h % 2 * MHD, (h % 2 + 1) * MHD)
                        ins = pe.matmul(PS[:, 2 + h % 2, h // 2 * MEM:(h // 2 + 1) * MEM],
                                        qmT[rows, h // 2, t * P:(t + 1) * P], mkT[rows, l, h // 2, :], start=True, stop=True)
                    ins.then_inc(sem("s_ready"), 1)

                def outputs(t):
                    pe.wait_ge(xp_act, JOB["p", l, t, 1] + 1)
                    if t >= 2:
                        pe.wait_ge(sem("on_ready"), l * TT + t - 1)
                    for h in range(MH):
                        for m in range(MT):
                            q = h * MT + m
                            ins = pe.matmul(PS[:, 4 + t % 2, h * MHD:(h + 1) * MHD], pt[:, t % nb, q * P:(q + 1) * P],
                                            mv[:, l, m, h * MHD:(h + 1) * MHD], start=m == 0, stop=m == MT - 1)
                    ins.then_inc(sem("pv_ready"), 1)

                def out_job(t):
                    pe.wait_ge(sem("on_ready"), l * TT + t + 1)
                    b = job(("o", l, t))
                    for q in range(2):
                        ins = pe.transpose(PS[:, b, q * P:(q + 1) * P], on[:, t % 2, q * P:(q + 1) * P], ident[:])
                    ins.then_inc(xp_ready, 1)

                pe.wait_ge(xp_act, JOB[f"hm{l}", 1, 1] + 1)
                if l == 0:
                    pe.wait_ge(sem("cin_ready"), 2 * CT)
                else:
                    tile_out(pe, ("qs", 1, 1, TT - 1))
                scores(0)
                for t in range(TT):
                    pe.wait_ge(sem("p_ready"), l * TT + t + 1)
                    if t + 1 < TT:
                        scores(t + 1)
                    for h in range(2):
                        b = job(("p", l, t, h))
                        for q in range(4):
                            ins = pe.transpose(PS[:, b, q * P:(q + 1) * P], pb[:, t % nb, (4 * h + q) * P:(4 * h + q + 1) * P],
                                               ident[:])
                        ins.then_inc(xp_ready, 1)
                    if t >= 1:
                        out_job(t - 1)
                    outputs(t)
                out_job(TT - 1)

            def router(l):
                def logits(t):
                    pe.wait_ge(xp_act, JOB[f"ffn{l}", t, 1] + 1)
                    if t == 0:
                        pe.wait_ge(sem("router_in"), 64 * (l + 1))
                        tile_out(pe, ("wo", l, 3, TT - 1))
                    for k in range(KT):
                        ins = pe.matmul(PS[:, 2, t * 20:(t + 1) * 20].rearrange("p (a b) -> p a b", b=4),
                                        E["rT"][:, t % 2, k, :], rw[:, :, k, :], start=k == 0, stop=k == KT - 1)
                    ins.then_inc(sem("lg_ready"), 1)

                norm_jobs(f"ffn{l}", TT, lambda t: logits(t - 1) if t else None)
                logits(TT - 1)
                pe.wait_ge(sem("oh_ready"), l + 1)
                oh = E["rt"][:, 6, 0:32]
                pe.matmul(PS[:, 3, 0:32], lstrict[:], oh, start=True, stop=True)
                pe.matmul(PS[:, 3, 32:64], ones[:], oh, start=True, stop=True).then_inc(sem("cnt_ready"), 1)
                pe.wait_ge(sem("av_in"), l + 1)
                for t in range(TT):
                    ins = pe.matmul(PS[:, 4, 0:NSUB * 5], E["boh"][:, t, :], E["av"][:, t].rearrange("p a v -> p (a v)"),
                                    start=t == 0, stop=t == TT - 1)
                ins.then_inc(sem("slots_ready"), 1)

            def moe(l):
                def x_job(i, h):
                    sub, half = divmod(h, 2)
                    if half == 0:
                        pe.wait_ge(sem(f"xg_in{sub}"), 16 * (l * NMT + i + 1))
                    b = job(("x", l, i, h))
                    for k in range(4):
                        at_ = 4 * half + k
                        ins = pe.transpose(PS[:, b, k * P:(k + 1) * P], A["xg"][:, sub, at_:at_ + KT * (P - 1) + 1:KT], ident[:])
                    ins.then_inc(xp_ready, 1)

                def hidden(s):
                    i = s // EPG
                    n = CH["in", l, s]
                    if s % EPG == 0:
                        last = JOB["x", l, i, 3]
                        pe.wait_ge(xp_act, last + 1)
                        pe.wait_ge(xp_dve, JOB_LO[last])
                    chunk(n)
                    for sub in range(2):
                        if s >= 1:
                            pe.wait_ge(sem("act_ready"), 2 * (l * NSTEP + s - 1) + sub + 1)
                        o = PS[:, 6 + sub, 0:WC]
                        for k in range(KT):
                            xh = A["xth"][:, i % 2, k, sub * P:(sub + 1) * P]
                            xl = A["xtl"][:, i % 2, k, sub * P:(sub + 1) * P]
                            ws = slice(k * WC, (k + 1) * WC)
                            pe.matmul(o, xh, whi(n)[:, ws], start=k == 0, stop=False)
                            pe.matmul(o, xh, wlo(n)[:, ws], start=False, stop=False)
                            ins = pe.matmul(o, xl, whi(n)[:, ws], start=False, stop=k == KT - 1)
                        ins.then_inc(sem("hid_ready"), 1)

                def act_job(s):
                    pe.wait_ge(sem("act_ready"), 2 * (l * NSTEP + s) + 2)
                    b = job(("act", l, s))
                    for sub in range(2):
                        ins = pe.transpose(PS[:, b, sub * P:(sub + 1) * P], E["actm"][:, s % 2, sub, :], ident[:])
                    ins.then_inc(xp_ready, 1)

                def down(s):
                    i, e = divmod(s, EPG)
                    n = CH["dn", l, s]
                    chunk(n)
                    pe.wait_ge(xp_act, JOB["act", l, s] + 1)
                    pe.wait_ge(xp_dve, JOB_LO[JOB["act", l, s]])
                    if e == 0 and i >= 1:
                        pe.wait_ge(sem("y_out_a"), l * NMT + i)
                        pe.wait_ge(sem("y_out_v"), l * NMT + i)
                    for sub in range(2):
                        ah = A["ath"][:, s % 2, sub * P:(sub + 1) * P]
                        al = A["atl"][:, s % 2, sub * P:(sub + 1) * P]
                        for h in range(2):
                            o = bank(2 + 2 * sub + h)
                            ws = slice(h * 512, (h + 1) * 512)
                            pe.matmul(o, ah, whi(n)[:, ws], start=e == 0, stop=False)
                            pe.matmul(o, ah, wlo(n)[:, ws], start=False, stop=False)
                            ins = pe.matmul(o, al, whi(n)[:, ws], start=False, stop=e == EPG - 1)
                    ins.then_inc(sem("down_ready"), 1)

                pe.wait_ge(sem("idx_ready"), l + 1)
                for h in range(4):
                    x_job(0, h)
                for s in range(NSTEP + 1):
                    i, e = divmod(s, EPG)
                    if s < NSTEP and i + 1 < NMT:
                        x_job(i + 1, e)
                    if s >= 1:
                        act_job(s - 1)
                    if s < NSTEP:
                        hidden(s)
                    if s >= 1:
                        down(s - 1)

            pe.wait_ge(sem("consts"), 1)
            pe.wait_ge(sem("small_in"), 16 * 15)
            for c in range(CT):
                pe.transpose(PS[:, 0, c * (CW + 2):(c + 1) * (CW + 2)], E["cwr"][:, c * P:(c + 1) * P], ident[0:CW + 2, 0:CW + 2])
            pe.transpose(PS[:, 0, 256:262], gr[0:6, :], ident[0:6, 0:6]).then_inc(xp_ready, 1)
            norm_jobs("nmem", MT)
            last = JOB["nmem", MT - 1, 1]
            pe.wait_ge(xp_act, last + 1)
            pe.wait_ge(xp_dve, JOB_LO[last])
            for n in range(4):
                project(*CHUNKS[n], MT, KT, lambda k: E["mth"][:, k, :], lambda k: E["mtl"][:, k, :])
            for l in range(2):
                pe.wait_ge(sem("mk_ready"), l + 1)
                b = job(("mk", l))
                for pr in range(2):
                    for t in range(MT):
                        ins = pe.transpose(PS[:, b, pr * MEM + t * P:pr * MEM + (t + 1) * P],
                                           E["mkraw"][:, l, t, pr * P:(pr + 1) * P], ident[:])
                ins.then_inc(xp_ready, 1)

            def norm_done(name):
                last = JOB[name, TT - 1, 1]
                pe.wait_ge(xp_act, last + 1)
                pe.wait_ge(xp_dve, JOB_LO[last])

            norm_jobs("nmix0", TT)
            norm_done("nmix0")
            tile_out(pe, ("mem", 1, 1, MT - 1))
            for c in range(CT):
                if c == GLU_FIRST:
                    pe.wait_ge(sem("cin_ready"), 2 * c)
                    project("qm", 0, 0, TT, KT, hth, htl)
                    tile_out(pe, ("qm", 0, 0, TT - 1))
                n = CH["glu", 0, c]
                chunk(n)
                for h in range(2):
                    s = 2 * c + h
                    if s >= 2:
                        pe.wait_ge(sem("cin_ready"), s - 1)
                    for g in range(2):
                        o = bank(2 + 2 * (s % 2) + g)
                        for k in range(KT):
                            ws = slice(k * WC + g * P, k * WC + (g + 1) * P)
                            q = slice(h * 512, (h + 1) * 512)
                            pe.matmul(o, whi(n)[:, ws], hth(k)[:, q], start=k == 0, stop=False)
                            pe.matmul(o, whi(n)[:, ws], htl(k)[:, q], start=False, stop=False)
                            ins = pe.matmul(o, wlo(n)[:, ws], hth(k)[:, q], start=False, stop=k == KT - 1)
                    ins.then_inc(sem("glu_ready"), 1)
            head_jobs("hm0")
            memory_attention(0)
            pe.wait_ge(sem("p_ready"), TT)
            for c in range(CT):
                pe.wait_ge(sem("conv_ready"), c + 1)
                for h in range(2):
                    ins = pe.matmul(bank(6 + h), ones[:], E["cv"][:, c, h * 512:(h + 1) * 512], start=c == 0, stop=c == CT - 1)
            ins.then_inc(sem("mean_ready"), 1)
            for c in range(CT):
                pe.wait_ge(sem("xsq_ready"), c + 1)
                for h in range(2):
                    ins = pe.matmul(bank(2 + h), ones[:], C["pb0"][:, c % 2, h * 512:(h + 1) * 512], start=c == 0,
                                    stop=c == CT - 1)
                ins.then_inc(sem("var_used"), 1)
            pe.wait_ge(sem("ln_lo"), CT)
            pe.wait_ge(xp_dve, JOB_LO[JOB["o", 0, TT - 1]])
            for c in range(4):
                project("wo", 0, c, TT, KT, hth, htl)
            router(0)
            moe(0)
            norm_jobs("nkv", TT)
            norm_done("nkv")
            pe.wait_ge(sem("y_out_v"), NMT)
            pe.wait_ge(sem("y_out_a"), NMT)
            for j in range(2):
                project("kv", 0, j, TT, KT, hth, htl)
                project("kv", 0, 2 + j, TT, KT, hth, htl)
                head_jobs(f"hk{j}")
            project("qm", 1, 0, TT, KT, hth, htl)
            project("qs", 1, 0, TT, KT, hth, htl)
            head_jobs("hm1")
            project("qs", 1, 1, TT, KT, hth, htl)
            head_jobs("hq0")
            memory_attention(1)
            head_jobs("hq1")
            pe.wait_ge(xp_act, JOB["hq1", 1, 1] + 1)
            kT, V, qT = E["kT"], E["V"], C["qT"]
            pe.wait_ge(sem("on_ready"), 2 * TT)
            pe.wait_ge(xp_act, JOB["o", 1, TT - 1] + 1)
            pe.wait_ge(xp_dve, JOB_LO[JOB["o", 1, TT - 1]])

            def logits(n):
                head, i = divmod(n, NSB)
                b, q0, w, diag = SB_STEPS[i]
                if n >= ZB:
                    pe.wait_ge(sem("wgt_ready"), n - ZB + 1)
                ins = pe.matmul(PS[:, n % ZB, 0:w], kT[:, head, b * P:(b + 1) * P], qT[:, head, q0:q0 + w], start=True,
                                stop=not diag, skip_group_check=True)
                if diag:
                    ins = pe.matmul(PS[:, n % ZB, 0:P], ident[:], negm[:], start=False, stop=True, skip_group_check=True)
                ins.then_inc(sem("z_ready"), 1)

            def remainders(n):
                head, i = divmod(n, NSB)
                b, q0, w, diag = SB_STEPS[i]
                pe.wait_ge(sem("sp_ready"), n + 1)
                d = P if diag else 0
                ins = pe.matmul(PS[:, n % ZB, 0:w], nuinc[:], C["sp"][:, n % 3, 0:w], start=False, stop=w == d,
                                skip_group_check=True)
                if w > d:
                    before = [m for m in range(head * NSB, n) if SB_STEPS[m % NSB][0] == b + 1 and
                              SB_STEPS[m % NSB][1] // 512 == q0 // 512]
                    pe.wait_ge(sem("sum_ready"), SUMS(before[-1]))
                    ins = pe.matmul(PS[:, n % ZB, d:w], nones[:], B["lfsum"][:, (b + 1) % 2, q0 + d:q0 + w], start=False,
                                    stop=True, skip_group_check=True)
                ins.then_inc(sem("r_ready"), 1)

            def values(n):
                head, i = divmod(n, NSB)
                b, q0, w, diag = SB_STEPS[i]
                h = q0 // 512
                pe.wait_ge(sem("wgt_ready"), n + 1)
                firsts = [j for j in range(NSB) if SB_STEPS[j][1] // 512 == h]
                if i == 0 and head >= 2:
                    pe.wait_ge(sem("sbo_lo"), 2 * (head - 1))
                c0 = q0 - h * 512
                ins = pe.matmul(PS[:, 4 + 2 * (head % 2) + h, c0:c0 + w], V[:, b, head * SHD:(head + 1) * SHD],
                                B["wgt"][:, n % 2, 0:w], start=i == firsts[0], stop=i == firsts[-1], skip_group_check=True)
                ins.then_inc(sem("av_ready"), 1)

            total = SH * NSB
            for n in range(total + 3):
                if n < total:
                    logits(n)
                if 2 <= n <= total + 1:
                    values(n - 2)
                if 1 <= n <= total:
                    remainders(n - 1)
            pe.wait_ge(sem("sbo_lo"), 2 * SH)
            for c in range(4):
                project("wo", 1, c, TT, 6, hth, htl)
            router(1)
            moe(1)


def SUMS(n):
    head, i = divmod(n, NSB)
    with_sum = [b > 0 for b, _, _, _ in SB_STEPS]
    return head * sum(with_sum) + sum(with_sum[:i + 1])


_INS = ["x", "mem", "mem_norm_g", "mix_norm_g", "ffn_norm_g", "w_in_a", "conv_w", "conv_ln_g", "conv_ln_b", "w_out_a",
        "w_in_b", "sb_q_norm_g", "w_out_b", "kv_norm_g", "w_kv", "sb_k_norm_g", "w_mem_kv", "mem_q_norm_g",
        "mem_k_norm_g", "router_g_w", "router_g_b", "router_e_w", "router_e_b", "moe_w_in", "moe_w_down"]


def kernel(**inputs):
    import concourse.bacc as bacc
    from concourse.bass_utils import run_bass_kernel_spmd

    nc = bacc.Bacc("TRN2", target_bir_lowering=False, num_devices=1)
    arrays, args = {}, {}
    for name in _INS:
        v = np.ascontiguousarray(inputs[name])
        arrays[f"in_{name}"] = v
        args[name] = nc.dram_tensor(f"in_{name}", v.shape, mybir.dt.from_np(v.dtype), kind="ExternalInput").ap()
    out = nc.dram_tensor("out_0", (1, T, D), F32, kind="ExternalOutput").ap()
    trunk(nc, args, out)
    r = run_bass_kernel_spmd(nc, [arrays], core_ids=[0])
    return r.results[0]["out_0"]
```

```python
from contextlib import ExitStack

import numpy as np

import concourse.bass as bass
from concourse import mybir

F32 = mybir.dt.float32
F32R = mybir.dt.float32r
BF16 = mybir.dt.bfloat16
I32 = mybir.dt.int32
ALU = mybir.AluOpType
ACT = mybir.ActivationFunctionType
AX = mybir.AxisListType.X

P = 128
D = 1024
T = 1024
TT = T // P
KT = D // P
MEM = 256
MT = MEM // P
MH, MHD = 4, 64
MW = MH * MHD
CC = D - MW
CT = CC // P
CW = 31
PE_TAPS = [0, 4, 4, 4, 6, 6]
HM0_AT, ATT_AT = (2, 24), (4, 27)
SH, SHD = 4, 128
SW = SH * SHD
G, EPG, HID = 4, 4, 128
EPS = 1e-6
WC = 256
MTILE = 256
NMT = (T - G) // MTILE + G
NSUB = NMT * MTILE // P
NSTEP = NMT * EPG
BIG = 1.0e30

CHUNKS = [("mem", l, c) for l in range(2) for c in range(2)]
GLU_FIRST = 3
CHUNKS += [("glu", 0, c) for c in range(GLU_FIRST)] + [("qm", 0, 0)] + [("glu", 0, c) for c in range(GLU_FIRST, CT)]
CHUNKS += [("wo", 0, c) for c in range(4)]
_moe = lambda l: [("in", l, 0)] + [x for s in range(1, NSTEP) for x in (("in", l, s), ("dn", l, s - 1))] + [("dn", l, NSTEP - 1)]
CHUNKS += _moe(0)
CHUNKS += [("kv", 0, c) for c in (0, 2, 1, 3)] + [("qm", 1, 0), ("qs", 1, 0), ("qs", 1, 1)]
CHUNKS += [("wo", 1, c) for c in range(4)] + _moe(1)
CH = {k: n for n, k in enumerate(CHUNKS)}
RAW = 3
SLOT, PREV = [], []
RSLOT, RPREV = [], []
_last, _turn = {}, 0
for _n, (_kind, _l, _c) in enumerate(CHUNKS):
    _inmoe = _kind in ("in", "dn")
    _turn = (_turn + 1) % (3 if _inmoe else 2)
    SLOT.append(_turn)
    if _turn == 2 and (_kind, _c) in (("in", 0), ("in", 1), ("dn", 0)) and _last.get(2, -1) < CH[("wo", _l, 3)]:
        PREV.append(CH[("wo", _l, 3)])
    else:
        PREV.append(_last.get(_turn, -1))
    _last[_turn] = _n
_last, _turn = {}, 0
for _n, (_kind, _l, _c) in enumerate(CHUNKS):
    _turn = (_turn + 1) % (3 if _kind in ("in", "dn") else 2)
    RSLOT.append(_turn)
    RPREV.append(_last.get(_turn, -1))
    if _turn == 2 and _last.get(2, -1) < CH[("in", _l, 0)]:
        RPREV[-1] = -1
    _last[_turn] = _n
LO_P = [0 if k in ("dn", "kv", "qs") or (k, l) == ("qm", 1) else (768 if c else 1024) if k == "in" else 2048
        for k, l, c in CHUNKS]
LO_P_CNT = [sum(x > 0 for x in LO_P[:n + 1]) for n in range(len(CHUNKS))]
LO_V_CNT = [sum(x < 2048 for x in LO_P[:n + 1]) for n in range(len(CHUNKS))]

JOBS = []


def _nt(name, tiles, lo):
    return [((name, t, h), lo) for t in range(tiles) for h in range(2)]


def _moe_jobs(l):
    out = [(("x", l, 0, h), True) for h in range(4)]
    for s in range(NSTEP + 1):
        i, e = divmod(s, EPG)
        if s < NSTEP and i + 1 < NMT:
            out.append((("x", l, i + 1, e), True))
        if s >= 1:
            out.append((("act", l, s - 1), True))
    return out


def _attn_jobs(l):
    out = []
    for t in range(TT + 1):
        if t < TT:
            out += [(("p", l, t, h), False) for h in range(2)]
        if t >= 1:
            out.append((("o", l, t - 1), True))
    return out


def _hn(name):
    return [((name, pr, h), False) for pr in range(2) for h in range(2)]


JOBS += _nt("nmem", MT, True) + [(("cw",), False)] + _nt("nmix0", TT, True) + [(("mk", 0), False), (("mk", 1), False)]
JOBS += _hn("hm0") + _attn_jobs(0) + _nt("ffn0", TT, False) + _moe_jobs(0)
JOBS += _nt("nkv", TT, True) + _hn("hk0") + _hn("hk1")
JOBS += _hn("hm1") + _hn("hq0") + _attn_jobs(1) + _hn("hq1") + _nt("ffn1", TT, False) + _moe_jobs(1)
JOB = {k: n for n, (k, _) in enumerate(JOBS)}
JOB_LO = [sum(d for _, d in JOBS[:n + 1]) for n in range(len(JOBS))]

TILES = [(("mem", l, c, t), False) for l in range(2) for c in range(2) for t in range(MT)]
TILES += [(("qm", 0, 0, t), False) for t in range(TT)]
TILES += [(("wo", 0, c, t), True) for c in range(4) for t in range(TT)]
TILES += [(("kv", 0, c, t), False) for c in (0, 2, 1, 3) for t in range(TT)]
TILES += [(("qm", 1, 0, t), False) for t in range(TT)] + [(("qs", 1, c, t), False) for c in range(2) for t in range(TT)]
TILES += [(("wo", 1, c, t), True) for c in range(4) for t in range(TT)]
TILE = {k: n for n, (k, _) in enumerate(TILES)}
TILE_CNT = [sum(TILES[m][1] == TILES[n][1] for m in range(n + 1)) for n in range(len(TILES))]

SB_STEPS = []
for _b in range(TT - 1, -1, -1):
    for _h in (1, 0):
        _q0 = max(_b * P, _h * 512)
        if _q0 < (_h + 1) * 512:
            SB_STEPS.append((_b, _q0, (_h + 1) * 512 - _q0, _q0 == _b * P))
NSB = len(SB_STEPS)
LN_EXP_SET = 6
ZB = 4


def trunk(nc, a, out):
    ctx = ExitStack()
    with ctx:
        def sb(name, shape, dt=F32, stack=ctx):
            return stack.enter_context(nc.sbuf_tensor(name, shape, dt))

        sems = {}

        def sem(name):
            if name not in sems:
                sems[name] = ctx.enter_context(nc.semaphore(name))
            return sems[name]

        def region(name, *sets):
            t, most = {}, 0
            for tensors in sets:
                with ExitStack() as shelf:
                    for n, s, dt in tensors:
                        t[n] = sb(n, s, dt, shelf)
                most = max(most, sum(int(np.prod(s[1:])) * (2 if dt == BF16 else 4) for _, s, dt in tensors))
            sb(name, [P, -(-most // 4)])
            return t

        hn = [nc.dram_tensor(f"hn{l}", [T, D], F32).ap() for l in range(2)]
        ybuf = [nc.dram_tensor(f"ybuf{l}", [NSUB * P, D], F32).ap() for l in range(2)]
        xsave = nc.dram_tensor("xsave", [T, D], F32).ap()

        wraw_ = [sb(f"wraw{i}", [P, 2048]) for i in range(2)]
        whi_ = [sb(f"whi{i}", [P, 2048], F32R) for i in range(2)]
        wlo_ = [sb(f"wlo{i}", [P, 2048], F32R) for i in range(2)]
        hb = sb("hb", [P, 2048])
        gkv = sb("gkv", [P, KT])
        gmix1 = sb("gmix1", [P, KT])
        gb = sb("gb", [P, D])
        mkT = sb("mkT", [P, 2, 2, 2 * MEM])
        mv = sb("mv", [P, 2, MT, MW])
        junk = sb("junk", [P, 256], BF16)
        ident = sb("ident", [P, P])
        ones = sb("ones", [P, P])
        nones = sb("nones", [P, P])
        nuinc = sb("nuinc", [P, P])
        lstrict = sb("lstrict", [P, P])
        negm = sb("negm", [P, P])
        iota = sb("iota", [P, P])
        tokid = sb("tokid", [P, TT])
        desc = sb("desc", [P, 4])
        iota_i = junk[:].bitcast(I32)
        cw = sb("cw", [P, CT, CW + 2])
        gcol = sb("gcol", [P, 8])
        rw = sb("rw", [P, KT, 20])
        rbias = sb("rbias", [P, 20])
        ssq = sb("ssq", [P, 32])
        rs = sb("rs", [P, 32])
        ssqx = sb("ssqx", [P, TT])
        rsx = sb("rsx", [P, TT])
        nx = sb("nx", [P, 32])
        ny = sb("ny", [P, 32])
        nw = sb("nw", [P, 32])
        eps_t = sb("eps_t", [P, 1])
        mx = sb("mx", [P, TT, 4])
        nmx = sb("nmx", [P, TT, 4])
        psm = sb("psm", [P, TT, 4])
        pri = sb("pri", [P, TT, 4])
        idx = sb("idx", [P, NSUB], I32)
        slot_i = sb("slot_i", [P, TT], I32)
        gates = sb("gates", [P, NSUB, 4])
        grp = sb("grp", [P, 8], I32)
        A = region("region_a", [("hth_a", [P, 6, T], F32R), ("htl_a", [P, 6, T], F32R)],
                   [("xth", [P, 2, KT, MTILE], F32R), ("xtl", [P, 2, KT, MTILE], F32R), ("ath", [P, 2, 2 * P], F32R),
                    ("atl", [P, 2, 2 * P], F32R), ("xg", [P, 2, D], F32)],
                   [("yg", [P, TT, D], F32)])
        B = region("region_b", [("hth_b", [P, 2, T], F32R), ("htl_b", [P, 2, T], F32R)],
                   [("whi2", [P, 2048], F32R), ("wlo2", [P, 2048], F32R)],
                   [("lfsum", [P, 2, T], F32), ("wgt", [P, 2, 512], F32), ("on1", [P, 2, MW], F32)])
        C = region("region_c", [("X", [P, TT, D], F32)],
                   [("qmT0", [P, 2, T], F32), ("pb0", [P, 2, D], F32), ("pt0", [P, 2, D], F32), ("on0", [P, 2, MW], F32),
                    ("sg", [P, 2, 512], F32)],
                   [("qT", [P, SH, T], F32), ("qmT1", [P, 2, T], F32), ("hb2", [P, 2048], F32)],
                   [("pad_c", [P, SH, T], F32), ("lt", [P, 3, 512], F32), ("sp", [P, 3, 512], F32)])
        E = region("region_e", [("memb", [P, MT, D], F32), ("mth", [P, KT, MEM], F32R), ("mtl", [P, KT, MEM], F32R),
                    ("cwr", [CW + 2, CC], F32), ("gr", [8, P], F32), ("mkraw", [P, 2, MT, MW], F32)],
                   [("cin", [P, 2, T + CW - 1], F32), ("cv", [P, CT, T], F32)],
                   [("kT", [P, SH, T], F32), ("V", [P, TT, SW], F32)],
                   [("sgm", [P, 2, 2, P], F32), ("actm", [P, 2, 2, P], F32), ("rt", [P, 8, 160], F32),
                    ("rT", [P, 2, KT, P], F32), ("boh", [P, TT, P], F32), ("av", [P, TT, NSUB, 4], F32),
                     ("avi", [P, TT, NSUB], F32), ("aoh", [P, TT, NSUB], F32)],
                   [("pad_e", [P, 1024], F32), ("ysb", [P, 2, 2, D], F32), ("pad_e2", [P, 960], F32), ("wraw2", [P, 2048], F32)])
        X, gr = C["X"], E["gr"]
        C["pb1"] = C["hb2"][:, 0:D].rearrange("p (o n) -> p o n", o=1)
        C["pt1"] = C["hb2"][:, D:2 * D].rearrange("p (o n) -> p o n", o=1)
        PS = ctx.enter_context(nc.psum_tensor("PS", [P, 8, 512], F32))

        def bank(n):
            return PS[:, n, :]

        def banks(n):
            return PS[:, n:n + 2, :].rearrange("p a b -> p (a b)")

        def whi(n):
            return whi_[SLOT[n]] if SLOT[n] < 2 else B["whi2"]

        def wlo(n):
            return wlo_[SLOT[n]] if SLOT[n] < 2 else B["wlo2"]

        def wraw(n):
            return wraw_[RSLOT[n]] if RSLOT[n] < 2 else E["wraw2"]

        def width(n):
            kind, l, _ = CHUNKS[n]
            return 1024 if kind == "dn" else 6 * WC if (kind, l) == ("wo", 1) else 2048

        def hth(k):
            return A["hth_a"][:, k, :] if k < 6 else B["hth_b"][:, k - 6, :]

        def htl(k):
            return A["htl_a"][:, k, :] if k < 6 else B["htl_b"][:, k - 6, :]

        def halves(name, t, h):
            tok = slice(t * P, t * P + P)
            if name == "nmem":
                return [(0, 4, E["mth"][:, 4 * h:4 * h + 4, tok], E["mtl"][:, 4 * h:4 * h + 4, tok])]
            if h == 0:
                return [(0, 4, A["hth_a"][:, 0:4, tok], A["htl_a"][:, 0:4, tok])]
            return [(0, 2, A["hth_a"][:, 4:6, tok], A["htl_a"][:, 4:6, tok]),
                    (2, 4, B["hth_b"][:, :, tok], B["htl_b"][:, :, tok])]

        w_raw = [sem(f"w_raw{i}") for i in range(RAW)]
        w_hi, w_lo_p, w_lo_v = sem("w_hi"), sem("w_lo_p"), sem("w_lo_v")
        xp_ready, xp_act, xp_dve = sem("xp_ready"), sem("xp_act"), sem("xp_dve")
        pj_ready, pj_a, pj_v = sem("pj_ready"), sem("pj_a"), sem("pj_v")
        v_step, a_step, p_step = sem("v_step"), sem("a_step"), sem("p_step")
        h_ready = sem("h_ready")
        NT_BASE = {"nmem": 0, "nmix0": MT, "ffn0": MT + TT, "nkv": MT + 2 * TT, "ffn1": MT + 3 * TT}
        SQ_BASE = {"nmem": 0, "nmix0": MT, "ffn0": MT + TT, "nkv": MT + 2 * TT, "ffn1": MT + 3 * TT}
        GB = {"nmem": 1, "nmix0": 2, "ffn0": 3, "ffn1": 4}
        HN = {"hm0": 0, "hk0": 1, "hk1": 2, "hm1": 3, "hq0": 4, "hq1": 5}
        HN_CHUNK = {"hm0": ("qm", 0, 0), "hk0": ("kv", 0, 0), "hk1": ("kv", 0, 1), "hq0": ("qs", 1, 0),
                    "hq1": ("qs", 1, 1), "hm1": ("qm", 1, 0)}

        HB_BEFORE = {"nmix0": ("nmem", MT - 1, 1), "ffn0": ("hm0", 1, 1), "nkv": ("ffn0", TT - 1, 1),
                     "ffn1": ("hq1", 1, 1)}

        def diagonals(c):
            return C["pb0"][:, c % 2, 0:PE_TAPS[c] * P].rearrange("p (j n) -> p j n", j=PE_TAPS[c])

        def swish(n):
            return C["pb0"][:, n // 2 % 2, n % 2 * 512:(n % 2 + 1) * 512]

        def score_banks(l, t):
            return 6 if l == 1 and t % 2 else 2

        def logits_half(h):
            return E["actm" if h else "sgm"][0:20].rearrange("p a b n -> p (a b n)")

        def raw_heads(name):
            return C["hb2"] if name == "hq0" else hb

        def chunk_done(eng, n):
            kind, l, c = CHUNKS[n]
            if kind == "glu":
                eng.wait_ge(sem("glu_ready"), 2 * c + 2)
            elif kind == "in":
                eng.wait_ge(sem("hid_ready"), 2 * (l * NSTEP + c) + 2)
            elif kind == "dn":
                eng.wait_ge(sem("down_ready"), l * NSTEP + c + 1)
            else:
                eng.wait_ge(pj_ready, TILE[kind, l, c, (MT if kind == "mem" else TT) - 1] + 1)

        def weight_gain(n):
            kind, l, _ = CHUNKS[n]
            return gkv if kind == "kv" else gmix1 if l == 1 and kind in ("qm", "qs") else None

        def lo_made(eng, n):
            if LO_P[n]:
                eng.wait_ge(w_lo_p, LO_P_CNT[n])
            if LO_P[n] < 2048:
                eng.wait_ge(w_lo_v, LO_V_CNT[n])

        def tile_out(eng, key):
            eng.wait_ge(pj_v if TILES[TILE[key]][1] else pj_a, TILE_CNT[TILE[key]])

        block = ctx.enter_context(nc.Block())

        @block.sync
        def _(sp):
            def weight_source(n, g=None):
                kind, l, c = CHUNKS[n]
                if kind == "mem":
                    return a["w_mem_kv"][l].rearrange("(p k) n -> p k n", k=KT)[:, :, c * WC:(c + 1) * WC]
                if kind == "qm":
                    w, at = (a["w_in_a"], 2 * CC) if l == 0 else (a["w_in_b"], SW)
                    return w[0].rearrange("(p k) n -> p k n", k=KT)[:, :, at:at + WC]
                if kind == "qs":
                    return a["w_in_b"][0].rearrange("(p k) n -> p k n", k=KT)[:, :, c * WC:(c + 1) * WC]
                if kind == "kv":
                    return a["w_kv"].rearrange("(p k) n -> p k n", k=KT)[:, :, c * WC:(c + 1) * WC]
                if kind == "wo":
                    w = a["w_out_a"] if l == 0 else a["w_out_b"]
                    return w[0].rearrange("(k p) n -> p k n", p=P)[:, :, c * WC:(c + 1) * WC]
                if kind == "in":
                    return a["moe_w_in"][l, bass.ds(g, 1), c % EPG].rearrange("o (p k) n -> p (o k n)", k=KT)
                return a["moe_w_down"][l, bass.ds(g, 1), c % EPG].rearrange("o p n -> p (o n)")

            def load_weight(n, g=None):
                kind, l, c = CHUNKS[n]
                if RPREV[n] >= 0:
                    lo_made(sp, RPREV[n])
                to = wraw(n)[:, 0:width(n)]
                if kind == "glu":
                    w = a["w_in_a"][0].rearrange("(p k) n -> p k n", k=KT)
                    to = to.rearrange("p (k h c) -> p k h c", k=KT, h=2)
                    src = w[:, :, 0:2 * CC].rearrange("p k (h c) -> p k h c", h=2)[:, :, :, c * P:(c + 1) * P]
                    sp.dma_start(to[:, :, 0, :], src[:, :, 0, :]).then_inc(w_raw[RSLOT[n]], 16)
                    sp.dma_start(to[:, :, 1, :], src[:, :, 1, :]).then_inc(w_raw[RSLOT[n]], 16)
                    return
                src = weight_source(n, g)
                if kind not in ("in", "dn"):
                    to = to.rearrange("p (k n) -> p k n", n=WC)
                sp.dma_start(to, src).then_inc(w_raw[RSLOT[n]], 16)

            def load_x(src):
                for t in range(TT):
                    sp.dma_start(X[:, t, :], src[t * P:(t + 1) * P, :]).then_inc(sem(f"x_in{t}"), 16)

            def moe_weights(l):
                sp.wait_ge(sem("grp_ready"), l + 1)
                g = None
                for s in range(NSTEP + 1):
                    if s < NSTEP:
                        before = g
                        if s % EPG == 0:
                            i = s // EPG
                            g = sp.value_load(grp[0:1, i:i + 1], min_val=0, max_val=G - 1)
                        load_weight(CH["in", l, s], g)
                    if s >= 1:
                        load_weight(CH["dn", l, s - 1], before if s % EPG == 0 and s < NSTEP else g)
                    i = (s - 7) // EPG
                    if s >= 7 and (s - 7) % EPG == 0 and i < NMT - 1:
                        store_y(l, i)

            def store_y(l, i):
                sp.wait_ge(sem("y_out_a"), l * NMT + i + 1)
                sp.wait_ge(sem("y_out_v"), l * NMT + i + 1)
                dst = ybuf[l].rearrange("(s p) n -> p s n", p=P)[:, 2 * i:2 * i + 2, :]
                sp.dma_start(dst, E["ysb"][:, i % 2, :, :]).then_inc(sem(f"y_stored{i % 2}"), 16)

            for t in range(MT):
                sp.dma_start(E["memb"][:, t, :], a["mem"][0, t * P:(t + 1) * P, :]).then_inc(sem("mem_in"), 16)
            load_weight(0)
            load_weight(1)
            load_x(a["x"][0])
            for n in range(2, CH["wo", 0, 2]):
                load_weight(n)
            sp.wait_ge(sem("ln_lo"), 2 * CT)
            load_x(a["x"][0])
            load_weight(CH["wo", 0, 2])
            load_weight(CH["wo", 0, 3])
            moe_weights(0)
            n0 = CH["kv", 0, 0]
            load_weight(n0)
            load_weight(n0 + 1)
            store_y(0, NMT - 1)
            for n in range(n0 + 2, CH["wo", 1, 2]):
                load_weight(n)
            sp.wait_ge(sem("sbo_lo"), 2 * SH)
            sp.wait_ge(sem("x_saved"), 16 * TT)
            load_x(xsave)
            load_weight(CH["wo", 1, 2])
            load_weight(CH["wo", 1, 3])
            moe_weights(1)
            store_y(1, NMT - 1)
            for t in range(TT):
                sp.wait_ge(sem("x_sum"), TT + t + 1)
                sp.dma_start(out[0, t * P:(t + 1) * P, :], X[:, t, :]).then_inc(sem("out_stored"), 16)
            sp.wait_ge(sem("out_stored"), 16 * TT)

        @block.gpsimd
        def _(pool):
            step = [0]

            def link(ins):
                step[0] += 1
                ins.then_inc(p_step, 1)
                pool.wait_ge(p_step, step[0])

            at = [0]

            def advance(n, ahead=2):
                while at[0] < len(CHUNKS) and at[0] <= n + ahead and PREV[at[0]] <= n - 1:
                    m = at[0]
                    at[0] += 1
                    w = min(LO_P[m], width(m))
                    if not w:
                        continue
                    pool.wait_ge(w_hi, m + 1)
                    pool.tensor_tensor(wlo(m)[:, 0:w], wraw(m)[:, 0:w], whi(m)[:, 0:w].bitcast(F32),
                                       ALU.subtract).then_inc(w_lo_p, 1)

            link(pool.memset(ident[:], 0.0))
            link(pool.affine_select(out=ident[:], in_=ident[:], compare_op=ALU.not_equal, fill=1.0, base=0,
                                    pattern=[[-1, P]], channel_multiplier=1))
            link(pool.memset(nuinc[:], -1.0))
            link(pool.affine_select(out=nuinc[:], in_=nuinc[:], compare_op=ALU.is_ge, fill=0.0, base=0,
                                    pattern=[[-1, P]], channel_multiplier=1))
            link(pool.memset(lstrict[:], 1.0))
            link(pool.affine_select(out=lstrict[:], in_=lstrict[:], compare_op=ALU.is_gt, fill=0.0, base=0,
                                    pattern=[[1, P]], channel_multiplier=-1))
            link(pool.memset(negm[:], 0.0))
            link(pool.affine_select(out=negm[:], in_=negm[:], compare_op=ALU.is_gt, fill=-BIG, base=0,
                                    pattern=[[1, P]], channel_multiplier=-1))
            link(pool.memset(ones[:], 1.0))
            link(pool.memset(mkT[:], 0.0))
            link(pool.memset(nones[:], -1.0))
            link(pool.memset(eps_t[:], EPS))
            for g in range(4):
                link(pool.memset(desc[:, g:g + 1], float(4 - g)))
            link(pool.iota(iota_i, pattern=[[1, P]], base=0, channel_multiplier=0))
            link(pool.tensor_copy(iota[:], iota_i))
            link(pool.iota(iota_i[:, 0:TT], pattern=[[P, TT]], base=0, channel_multiplier=1))
            pool.tensor_copy(tokid[:], iota_i[:, 0:TT]).then_inc(sem("consts"), 1)

            for n in range(CH["glu", 0, 0]):
                advance(n)
            pool.wait_ge(xp_act, JOB[("cw",)] + 1)
            for c in range(CT):
                advance(CH["glu", 0, c])
                if PE_TAPS[c]:
                    if c <= 2:
                        pool.wait_ge(xp_act, JOB["nmix0", TT - 1, 1] + 1)
                        pool.wait_ge(xp_dve, JOB_LO[JOB["nmix0", TT - 1, 1]])
                    if c >= 3:
                        pool.wait_ge(sem("base_ready"), c - 2)
                    d = diagonals(c)
                    pool.tensor_tensor(d, ident[:].unsqueeze(1).to_broadcast([P, PE_TAPS[c], P]),
                                       cw[:, c, 0:PE_TAPS[c]].unsqueeze(2).to_broadcast([P, PE_TAPS[c], P]), ALU.mult
                                       ).then_inc(sem("diag_ready"), 1)
            for n in range(CH["wo", 0, 0], CH["in", 0, 0]):
                advance(n)

            def moe(l):
                def gather_x(i, sub):
                    if i >= 1:
                        pool.wait_ge(xp_ready, JOB["x", l, i - 1, 2 * sub + 1] + 1)
                    pool.indirect_dma_start(out=A["xg"][:, sub, :], out_offset=None, in_=hn[l],
                                            in_offset=bass.IndirectOffsetOnAxis(ap=idx[:, 2 * i + sub:2 * i + sub + 1], axis=0)
                                            ).then_inc(sem(f"xg_in{sub}"), 16)

                for i in range(2):
                    pool.wait_ge(sem(f"hn_stored{i}"), 16 * (TT // 2) * (l + 1))
                pool.wait_ge(sem("idx_ready"), l + 1)
                gather_x(0, 0)
                gather_x(0, 1)
                advance(CH["in", l, 0], 0)
                gather_x(1, 0)
                for s in range(NSTEP):
                    i, e = divmod(s, EPG)
                    if e == 0 and i + 1 < NMT:
                        gather_x(i + 1, 1)
                    if e == 2 and i + 2 < NMT:
                        gather_x(i + 2, 0)
                    advance(CH["in", l, s])
                    if s >= 1:
                        advance(CH["dn", l, s - 1])
                advance(CH["dn", l, NSTEP - 1])
                for i in range(2):
                    pool.wait_ge(sem(f"y_stored{i}"), 16 * (l + 1) * ((NMT + 1 - i) // 2))
                for t in range(TT):
                    pool.indirect_dma_start(out=A["yg"][:, t, :], out_offset=None, in_=ybuf[l],
                                            in_offset=bass.IndirectOffsetOnAxis(ap=slot_i[:, t:t + 1], axis=0)
                                            ).then_inc(sem(f"yg_in{t}"), 16)

            moe(0)
            for n in range(CH["kv", 0, 0], CH["in", 1, 0]):
                advance(n)
            moe(1)

        @block.scalar
        def _(act):
            step = [0]

            def link(ins):
                step[0] += 1
                ins.then_inc(a_step, 1)
                act.wait_ge(a_step, step[0])

            at = [0]

            def advance(n, ahead=2):
                while at[0] < len(CHUNKS) and at[0] <= n + ahead and PREV[at[0]] <= n - 1:
                    m = at[0]
                    at[0] += 1
                    act.wait_ge(w_raw[RSLOT[m]], raw_count(m))
                    if PREV[m] >= 0:
                        chunk_done(act, PREV[m])
                    w = width(m)
                    gain = weight_gain(m)
                    if gain is None:
                        act.activation(whi(m)[:, 0:w], wraw(m)[:, 0:w], ACT.Copy).then_inc(w_hi, 1)
                    else:
                        act.wait_ge(sem("small_in"), 16 * 15)
                        for k in range(KT):
                            ws = slice(k * WC, (k + 1) * WC)
                            ins = act.activation(whi(m)[:, ws], wraw(m)[:, ws], ACT.Copy, scale=gain[:, k:k + 1])
                        ins.then_inc(w_hi, 1)

            def raw_count(n):
                return sum(32 if CHUNKS[m][0] == "glu" else 16 for m in range(n + 1) if RSLOT[m] == RSLOT[n])

            def load_gain(name):
                vec = {"nmem": a["mem_norm_g"], "nmix0": a["mix_norm_g"][0], "ffn0": a["ffn_norm_g"][0],
                       "ffn1": a["ffn_norm_g"][1]}[name]
                act.dma_start(gb[:], vec.partition_broadcast(P)).then_inc(sem("gain_in"), 16)

            def load_router(l):
                act.dma_start(rw[:, :, 0:4], a["router_g_w"][l].rearrange("(p k) g -> p k g", k=KT)).then_inc(sem("router_in"), 16)
                for g in range(G):
                    act.dma_start(rw[:, :, 4 + EPG * g:8 + EPG * g], a["router_e_w"][l, g].rearrange("(p k) e -> p k e", k=KT)
                                  ).then_inc(sem("router_in"), 16)
                act.dma_start(rbias[:, 0:4], a["router_g_b"][l].partition_broadcast(P)).then_inc(sem("router_in"), 16)
                act.dma_start(rbias[:, 4:20], a["router_e_b"][l].rearrange("g e -> (g e)").partition_broadcast(P)
                              ).then_inc(sem("router_in"), 16)

            def stats(name, source, tiles, ready):
                for t in range(tiles):
                    ready(t)
                    m = SQ_BASE[name] + t
                    if t == 0 and name in HB_BEFORE:
                        act.wait_ge(xp_ready, JOB[HB_BEFORE[name]] + 1)
                    if m >= 1:
                        act.wait_ge(sem("sq_ready"), m)
                    act.activation(hb[:, 0:D], source(t), ACT.Square, accum_out=ssqx[:, t:t + 1]).then_inc(sem("sq_ready"), 1)

            def out_hi(key, pairs):
                act.wait_ge(xp_ready, JOB[key] + 1)
                for dst, src in pairs:
                    ins = act.activation(dst, src, ACT.Copy)
                ins.then_inc(xp_act, 1)

            def half_view(key):
                return bank(JOB[key] % 2).rearrange("p (k t) -> p k t", k=4)

            def norm_out(name, tiles, next_gain=None):
                for t in range(tiles):
                    for h in range(2):
                        v = half_view((name, t, h))
                        out_hi((name, t, h), [(hi, v[:, k0:k1, :]) for k0, k1, hi, _ in halves(name, t, h)])
                if next_gain:
                    load_gain(next_gain)

            def tile_copy(key, dst):
                act.wait_ge(pj_ready, TILE[key] + 1)
                b = 2 + TILE[key] % 4
                act.activation(dst, PS[:, b, 0:WC], ACT.Copy).then_inc(pj_a, 1)

            def heads_out(name, gain, dst):
                for pr in range(2):
                    for h in range(2):
                        key = (name, pr, h)
                        act.wait_ge(xp_ready, JOB[key] + 1)
                        act.activation(dst(pr, h), bank(JOB[key] % 2), ACT.Copy, scale=gcol[:, gain:gain + 1]
                                       ).then_inc(xp_act, 1)

            def memory_attention(l):
                pb, pt, nb = C[f"pb{l}"], C[f"pt{l}"], 2 - l
                k0 = 6 if l == 0 else 4
                for t in range(TT + 1):
                    if t < TT:
                        act.wait_ge(sem("s_max"), l * TT + t + 1)
                        if t >= nb:
                            act.wait_ge(xp_ready, JOB["p", l, t - nb, 1] + 1)
                        if (l, t) == (0, 1):
                            act.wait_ge(sem("base_ready"), CT - 1)
                        for h in range(MH):
                            ins = act.activation(pb[:, t % nb, h * MEM:(h + 1) * MEM],
                                                 banks(score_banks(l, t))[:, h * MEM:(h + 1) * MEM], ACT.Exp,
                                                 bias=nmx[:, t, h:h + 1], accum_out=psm[:, t, h:h + 1])
                        ins.then_inc(sem("p_ready"), 1)
                        for h in range(2):
                            key = ("p", l, t, h)
                            if t >= nb and h == 0:
                                act.wait_ge(sem("pv_ready"), l * TT + t - nb + 1)
                            out_hi(key, [(pt[:, t % nb, h * 512:(h + 1) * 512], bank(JOB[key] % 2))])
                    if t >= 1:
                        key = ("o", l, t - 1)
                        v = bank(JOB[key] % 2)[:, 0:2 * P].rearrange("p (k t) -> p k t", k=2)
                        tok = slice((t - 1) * P, t * P)
                        dst = B["hth_b"][:, :, tok] if l == 0 else A["hth_a"][:, 4:6, tok]
                        out_hi(key, [(dst, v)])

            def logits_out(l, h):
                act.wait_ge(sem("lg_ready"), l * TT + 4 * h + 4)
                act.activation(logits_half(h), PS[0:20, 2 + h, :], ACT.Copy).then_inc(sem("lg_out"), 1)

            def router_and_dispatch(l):
                for t in range(TT):
                    act.wait_ge(h_ready, NT_BASE[f"ffn{l}"] + t + 1)
                    act.dma_start(hn[l][t * P:(t + 1) * P, :], hb[:, (t % 2) * D:(t % 2) * D + D]
                                  ).then_inc(sem(f"hn_stored{t % 2}"), 16)
                    for h in range(2):
                        key = (f"ffn{l}", t, h)
                        if h == 0 and t >= 2:
                            act.wait_ge(sem("lg_ready"), l * TT + t - 1)
                        out_hi(key, [(E["rT"][:, t % 2, 4 * h:4 * h + 4, :], half_view(key))])
                    if t == 5:
                        logits_out(l, 0)
                logits_out(l, 1)
                act.wait_ge(sem("dg_ready"), l + 1)
                act.activation(E["rt"][:, 1, 0:32], E["rt"][:, 1, 0:32], ACT.Exp).then_inc(sem("eg_ready"), 1)
                advance(CH["in", l, 0], 0)
                act.wait_ge(sem("dm_ready"), l + 1)
                act.activation(E["rt"][:, 2, 0:8], E["rt"][:, 2, 0:8], ACT.Exp).then_inc(sem("em_ready"), 1)
                if l == 0:
                    load_router(1)

            def moe(l):
                for h in range(4):
                    x_out(l, 0, h)
                for s in range(NSTEP + 1):
                    i, e = divmod(s, EPG)
                    if s < NSTEP and i + 1 < NMT:
                        x_out(l, i + 1, e)
                    if s >= 1:
                        key = ("act", l, s - 1)
                        out_hi(key, [(A["ath"][:, (s - 1) % 2, :], bank(JOB[key] % 2)[:, 0:2 * P])])
                        if s % EPG == 1 and s > EPG:
                            y_out(l, s // EPG - 1)
                    if s < NSTEP:
                        advance(CH["in", l, s])
                        for sub in range(2):
                            act.wait_ge(sem("hid_ready"), 2 * (l * NSTEP + s) + sub + 1)
                            if s >= 2 and sub == 0:
                                act.wait_ge(sem("act_ready"), 2 * (l * NSTEP + s - 1))
                            act.activation(E["sgm"][:, s % 2, sub, :], PS[:, 6 + sub, 0:HID],
                                           ACT.Silu).then_inc(sem("silu_ready"), 1)
                    if s >= 1:
                        advance(CH["dn", l, s - 1])
                y_out(l, NMT - 1)

            def x_out(l, i, h):
                key = ("x", l, i, h)
                sub, half = divmod(h, 2)
                out_hi(key, [(A["xth"][:, i % 2, 4 * half:4 * half + 4, sub * P:(sub + 1) * P], half_view(key))])

            def y_out(l, i):
                act.wait_ge(sem("down_ready"), l * NSTEP + EPG * (i + 1))
                if i >= 2 or l:
                    wait_stored(l, i)
                act.activation(E["ysb"][:, i % 2, 0, :], banks(2), ACT.Copy).then_inc(sem("y_out_a"), 1)

            def wait_stored(l, i):
                if i >= 2:
                    act.wait_ge(sem(f"y_stored{i % 2}"), 16 * (l * ((NMT + 1 - i % 2) // 2) + i // 2))

            def load_ln_exp():
                act.add_instruction(mybir.InstLoadActFuncSet(act_func_set_id=LN_EXP_SET, name=f"I-{nc.next_id()}",
                                                             engine=act.engine, ins=[], outs=[]))

            load_gain("nmem")

            stats("nmem", lambda t: E["memb"][:, t, :], MT, lambda t: act.wait_ge(sem("mem_in"), 16 * MT))
            act.dma_start(E["cwr"][0:CW, :], a["conv_w"][0]).then_inc(sem("small_in"), 16)
            act.dma_start(E["cwr"][CW:CW + 1, :], a["conv_ln_g"]).then_inc(sem("small_in"), 16)
            act.dma_start(E["cwr"][CW + 1:CW + 2, :], a["conv_ln_b"]).then_inc(sem("small_in"), 16)
            for l in range(2):
                for h in range(2):
                    act.dma_start(gr[l:l + 1, h * MHD:(h + 1) * MHD], a["mem_q_norm_g"][l:l + 1, :]).then_inc(sem("small_in"), 16)
                    act.dma_start(gr[2 + l:3 + l, h * MHD:(h + 1) * MHD], a["mem_k_norm_g"][l:l + 1, :]).then_inc(sem("small_in"), 16)
            act.dma_start(gr[4:5, :], a["sb_q_norm_g"]).then_inc(sem("small_in"), 16)
            act.dma_start(gr[5:6, :], a["sb_k_norm_g"].rearrange("(o n) -> o n", o=1)).then_inc(sem("small_in"), 16)
            act.dma_start(gkv[:], a["kv_norm_g"].rearrange("(p k) -> p k", k=KT)).then_inc(sem("small_in"), 16)
            act.dma_start(gmix1[:], a["mix_norm_g"][1].rearrange("(p k) -> p k", k=KT)).then_inc(sem("small_in"), 16)
            advance(0)
            norm_out("nmem", MT, "nmix0")
            act.wait_ge(xp_ready, JOB[("cw",)] + 1)
            act.activation(cw[:].rearrange("p c w -> p (c w)"), PS[:, JOB[("cw",)] % 2, 0:CT * (CW + 2)], ACT.Copy)
            act.activation(gcol[:, 0:6], PS[:, JOB[("cw",)] % 2, 256:262], ACT.Copy).then_inc(xp_act, 1)
            stats("nmix0", lambda t: X[:, t, :], TT, lambda t: act.wait_ge(sem(f"x_in{t}"), 16))
            for n in range(4):
                l, c = divmod(n, 2)
                advance(n)
                for t in range(MT):
                    tile_copy(("mem", l, c, t), E["mkraw"][:, l, t, :] if c == 0 else mv[:, l, t, :])
            act.wait_ge(sem("gcol_ready"), 1)

            def keys_out():
                for l in range(2):
                    act.wait_ge(xp_ready, JOB["mk", l] + 1)
                    act.wait_ge(sem("consts"), 1)
                    for h in range(2):
                        rows = slice(h * MHD, (h + 1) * MHD)
                        ins = act.activation(mkT[rows, l, :, h * MEM:(h + 1) * MEM],
                                             bank(JOB["mk", l] % 2)[rows, :].rearrange("p (a m) -> p a m", a=2), ACT.Copy,
                                             scale=gcol[rows, 2 + l:3 + l])
                    ins.then_inc(xp_act, 1)

            norm_out("nmix0", TT, "ffn0")
            load_router(0)
            for c in range(CT):
                if c == GLU_FIRST:
                    advance(CH["qm", 0, 0])
                    for t in range(TT):
                        tile_copy(("qm", 0, 0, t), hb[:, t * WC:(t + 1) * WC])
                advance(CH["glu", 0, c])
                for h in range(2):
                    s = 2 * c + h
                    act.wait_ge(sem("glu_ready"), s + 1)
                    if s >= 2:
                        act.wait_ge(sem("cin_ready"), s - 1)
                    act.activation(C["sg"][:, s % 2, :], bank(3 + 2 * (s % 2)), ACT.Sigmoid).then_inc(sem("sig_ready"), 1)
                    if s == 0:
                        keys_out()
            heads_out("hm0", 0, lambda pr, h: C["qmT0"][:, pr, h * 512:(h + 1) * 512])
            memory_attention(0)
            advance(CH["wo", 0, 0] - 1)
            load_ln_exp()
            for c in range(CT):
                act.wait_ge(sem("xc_ready"), c + 1)
                if c >= 2:
                    act.wait_ge(sem("var_used"), c - 1)
                act.activation(C["pb0"][:, c % 2, :], E["cv"][:, c, :], ACT.Square).then_inc(sem("xsq_ready"), 1)
            act.wait_ge(sem("var_used"), CT)
            link(act.activation(C["pt0"][:, 0, :], banks(2), ACT.Ln, scale=1.0 / CC, bias=eps_t[:]))
            act.activation(C["pt0"][:, 1, :], C["pt0"][:, 0, :], ACT.Exp, scale=-0.5).then_inc(sem("std_ready"), 1)
            for n in range(2 * CT):
                h, c = divmod(n, CT)
                q = slice(h * 512, (h + 1) * 512)
                act.wait_ge(sem("y0_ready"), n + 1)
                if n >= 4:
                    act.wait_ge(sem("ln_lo"), n - 3)
                link(act.activation(swish(n), E["cv"][:, c, q], ACT.Silu, scale=cw[:, c, CW:CW + 1],
                                    bias=cw[:, c, CW + 1:CW + 2]))
                act.activation(A["hth_a"][:, c, q], swish(n), ACT.Copy).then_inc(sem("ln_hi"), 1)
            for c in range(4):
                advance(CH["wo", 0, c])

            def ffn(l):
                stats(f"ffn{l}", lambda t: X[:, t, :], TT, lambda t: tile_out(act, ("wo", l, 3, t)))
                router_and_dispatch(l)
                moe(l)

            ffn(0)
            def saved(t):
                act.wait_ge(sem("x_sum"), t + 1)
                act.dma_start(xsave[t * P:(t + 1) * P, :], X[:, t, :]).then_inc(sem("x_saved"), 16)

            stats("nkv", lambda t: X[:, t, :], TT, saved)
            norm_out("nkv", TT, "ffn1")
            for j in range(2):
                for c in (j, 2 + j):
                    advance(CH["kv", 0, c])
                    for t in range(TT):
                        tile_copy(("kv", 0, c, t), hb[:, t * WC:(t + 1) * WC] if c < 2 else
                                  E["V"][:, t, j * WC:(j + 1) * WC])
                heads_out(f"hk{j}", 5, lambda pr, h: E["kT"][:, 2 * j + pr, h * 512:(h + 1) * 512])
            act.wait_ge(sem("x_saved"), 16 * TT)

            def raw_out(kind, j, to):
                advance(CH[kind, 1, j])
                for t in range(TT):
                    tile_copy((kind, 1, j, t), to[:, t * WC:(t + 1) * WC])

            def queries_out(j):
                heads_out(f"hq{j}", 4, lambda pr, h: C["qT"][:, 2 * j + pr, h * 512:(h + 1) * 512])

            raw_out("qm", 0, hb)
            raw_out("qs", 0, C["hb2"])
            heads_out("hm1", 1, lambda pr, h: C["qmT1"][:, pr, h * 512:(h + 1) * 512])
            raw_out("qs", 1, hb)
            queries_out(0)
            memory_attention(1)
            queries_out(1)
            advance(CH["wo", 1, 0] - 1)

            def head_out(head):
                act.wait_ge(sem("av_ready"), (head + 1) * NSB)
                for h in range(2):
                    act.activation(A["hth_a"][:, head, h * 512:(h + 1) * 512], bank(4 + 2 * (head % 2) + h), ACT.Copy
                                   ).then_inc(sem("sbo_hi"), 1)

            load_ln_exp()
            for head in range(SH):
                for i in range(NSB + 1):
                    n = head * NSB + i
                    if i < NSB:
                        b, q0, w, diag = SB_STEPS[i]
                        lt = C["lt"][:, n % 3, 0:w]
                        act.wait_ge(sem("z_ready"), n + 1)
                        if n >= 3:
                            act.wait_ge(sem("sp_ready"), n - 2)
                        link(act.activation(lt, PS[:, n % ZB, 0:w], ACT.Abs))
                        link(act.activation(lt, lt, ACT.Exp, scale=-1.0))
                        act.activation(lt, lt, ACT.Ln, bias=1.0).then_inc(sem("l_ready"), 1)
                    if i >= 1:
                        m = n - 1
                        b, q0, w, diag = SB_STEPS[i - 1]
                        act.wait_ge(sem("r_ready"), m + 1)
                        if m >= 2:
                            act.wait_ge(sem("av_ready"), m - 1)
                        act.activation(B["wgt"][:, m % 2, 0:w], PS[:, m % ZB, 0:w], ACT.Exp).then_inc(sem("wgt_ready"), 1)
                    if i == 3 and head:
                        head_out(head - 1)
            head_out(SH - 1)
            for c in range(4):
                advance(CH["wo", 1, c])
            ffn(1)

        @block.vector
        def _(dve):
            step = [0]

            def link(ins):
                step[0] += 1
                ins.then_inc(v_step, 1)
                dve.wait_ge(v_step, step[0])

            at = [0]

            def advance(n, ahead=2):
                while at[0] < len(CHUNKS) and at[0] <= n + ahead and PREV[at[0]] <= n - 1:
                    m = at[0]
                    at[0] += 1
                    if LO_P[m] >= 2048:
                        continue
                    dve.wait_ge(w_hi, m + 1)
                    gain = weight_gain(m)
                    if gain is not None:
                        dve.wait_ge(sem("small_in"), 16 * 15)
                        for k in range(KT):
                            ws = slice(k * WC, (k + 1) * WC)
                            ins = dve.scalar_tensor_tensor(out=wlo(m)[:, ws], in0=wraw(m)[:, ws], scalar=gain[:, k:k + 1],
                                                           in1=whi(m)[:, ws].bitcast(F32), op0=ALU.mult, op1=ALU.subtract)
                        ins.then_inc(w_lo_v, 1)
                        continue
                    w = slice(LO_P[m], width(m))
                    dve.tensor_tensor(wlo(m)[:, w], wraw(m)[:, w], whi(m)[:, w].bitcast(F32),
                                      ALU.subtract).then_inc(w_lo_v, 1)

            def rsqrt(to, squares, n, count):
                x, y, t = nx[:, 0:n], ny[:, 0:n], nw[:, 0:n]
                link(dve.tensor_scalar(x, squares[:, 0:n], 1.0 / count, EPS, ALU.mult, ALU.add))
                link(dve.tensor_single_scalar(t.bitcast(I32), x.bitcast(I32), 1, ALU.arith_shift_right))
                link(dve.tensor_scalar(y.bitcast(I32), t.bitcast(I32), -1.0, 1597463007.0, ALU.mult, ALU.add))
                for k in range(3):
                    link(dve.tensor_tensor(t, y, y, ALU.mult))
                    link(dve.scalar_tensor_tensor(out=t, in0=t, scalar=-0.5, in1=x, op0=ALU.mult, op1=ALU.mult))
                    link(dve.scalar_tensor_tensor(out=y if k < 2 else to[:, 0:n], in0=t, scalar=1.5, in1=y,
                                                  op0=ALU.add, op1=ALU.mult))

            def out_lo(key, trios):
                dve.wait_ge(xp_act, JOB[key] + 1)
                for dst, src, hi in trios:
                    ins = dve.tensor_tensor(dst, src, hi.bitcast(F32), ALU.subtract)
                ins.then_inc(xp_dve, 1)

            def half_view(key):
                return bank(JOB[key] % 2).rearrange("p (k t) -> p k t", k=4)

            def norm(name, source, tiles, lo=True, gain=True):
                dve.wait_ge(sem("sq_ready"), SQ_BASE[name] + tiles)
                rsqrt(rsx, ssqx, tiles, D)
                if gain:
                    dve.wait_ge(sem("gain_in"), 16 * GB[name])
                if name in HB_BEFORE:
                    dve.wait_ge(xp_ready, JOB[HB_BEFORE[name]] + 1)

                def h_tile(t):
                    if t >= 2:
                        dve.wait_ge(xp_ready, JOB[name, t - 2, 1] + 1)
                        if not lo:
                            dve.wait_ge(sem(f"hn_stored{t % 2}"), 16 * (int(name[3]) * (TT // 2) + t // 2))
                    h = hb[:, (t % 2) * D:(t % 2) * D + D]
                    if gain:
                        dve.scalar_tensor_tensor(out=h, in0=source(t), scalar=rsx[:, t:t + 1], in1=gb[:], op0=ALU.mult,
                                                 op1=ALU.mult).then_inc(h_ready, 1)
                    else:
                        dve.tensor_scalar(h, source(t), rsx[:, t:t + 1], None, ALU.mult).then_inc(h_ready, 1)

                for t in range(tiles + 1):
                    if t < tiles:
                        h_tile(t)
                    if t >= 1 and lo:
                        for h in range(2):
                            v = half_view((name, t - 1, h))
                            out_lo((name, t - 1, h), [(lo_, v[:, k0:k1, :], hi) for k0, k1, hi, lo_ in halves(name, t - 1, h)])

            def head_norm(name):
                kind, l, c = HN_CHUNK[name]
                nh, hd = (MH, MHD) if kind == "qm" else (2, SHD)
                tile_out(dve, (kind, l, c, TT - 1))
                v = raw_heads(name)[:].rearrange("p (a d) -> p a d", d=hd)
                for i in range(TT * nh):
                    ins = dve.tensor_tensor_reduce(out=junk[:, (i * hd) % 256:(i * hd) % 256 + hd], in0=v[:, i, :], in1=v[:, i, :],
                                                   scale=1.0, scalar=0.0, op0=ALU.mult, op1=ALU.add, accum_out=ssq[:, i:i + 1])
                    if (i + 1) * hd % 256 == 0:
                        link(ins)
                rsqrt(rs, ssq, TT * nh, hd)
                dve.tensor_tensor(v, v, rs[:, 0:TT * nh].unsqueeze(2).to_broadcast([P, TT * nh, hd]), ALU.mult
                                  ).then_inc(sem("hn_ready"), 1)

            def attention_steps(l):
                on = C["on0"] if l == 0 else B["on1"]

                def maxima(t):
                    dve.wait_ge(sem("s_ready"), l * TT + t + 1)
                    link(dve.tensor_reduce(mx[:, t, :], banks(score_banks(l, t)).rearrange("p (h m) -> p h m", h=MH), AX, ALU.max))
                    dve.tensor_scalar(nmx[:, t, :], mx[:, t, :], -1.0, None, ALU.mult).then_inc(sem("s_max"), 1)

                def outputs(t):
                    dve.wait_ge(sem("p_ready"), l * TT + t + 1)
                    link(dve.reciprocal(pri[:, t, :], psm[:, t, :]))
                    dve.wait_ge(sem("pv_ready"), l * TT + t + 1)
                    if t >= 2:
                        dve.wait_ge(xp_ready, JOB["o", l, t - 2] + 1)
                    dve.tensor_tensor(on[:, t % 2, :].rearrange("p (h d) -> p h d", h=MH),
                                      PS[:, 4 + t % 2, 0:MW].rearrange("p (h d) -> p h d", h=MH),
                                      pri[:, t, :].unsqueeze(2).to_broadcast([P, MH, MHD]), ALU.mult
                                      ).then_inc(sem("on_ready"), 1)

                def lows(t):
                    key = ("o", l, t)
                    v = bank(JOB[key] % 2)[:, 0:2 * P].rearrange("p (k t) -> p k t", k=2)
                    tok = slice(t * P, (t + 1) * P)
                    hi, lo = (B["hth_b"][:, :, tok], B["htl_b"][:, :, tok]) if l == 0 else \
                        (A["hth_a"][:, 4:6, tok], A["htl_a"][:, 4:6, tok])
                    out_lo(key, [(lo, v, hi)])

                steps = [lambda: maxima(0)]
                for t in range(TT):
                    if t + 1 < TT:
                        steps.append(lambda t=t: maxima(t + 1))
                    if t >= 1:
                        steps.append(lambda t=t: lows(t - 1))
                    steps.append(lambda t=t: outputs(t))
                return steps + [lambda: lows(TT - 1)]

            def dispatch(l):
                rt = E["rt"]

                def r(n, k, shape=None):
                    v = rt[:, n, 0:k]
                    return v if shape is None else v.rearrange(shape[0], **shape[1])

                dve.wait_ge(sem("lt_ready"), l + 1)
                dve.wait_ge(sem("router_in"), 112 * (l + 1))
                lg = rt[:, 0, 0:160].rearrange("p (t c) -> p t c", t=TT)
                link(dve.tensor_tensor(lg, PS[:, 5, 0:160].rearrange("p (t c) -> p t c", t=TT),
                                       rbias[:].unsqueeze(1).to_broadcast([P, TT, 20]), ALU.add))
                glog = lg[:, :, 0:4]
                dg = rt[:, 1, 0:32].rearrange("p (t g) -> p t g", g=4)
                gmax, m1, m2, mm = (rt[:, 3, 8 * k:8 * k + 8] for k in range(4))
                oh = rt[:, 4, 0:32].rearrange("p (t g) -> p t g", g=4)
                o1 = rt[:, 4, 32:64].rearrange("p (t g) -> p t g", g=4)
                o2 = rt[:, 4, 64:96].rearrange("p (t g) -> p t g", g=4)
                pr = rt[:, 4, 96:128].rearrange("p (t g) -> p t g", g=4)
                sel = rt[:, 5, 0:32].rearrange("p (t g) -> p t g", g=4)
                sel2 = rt[:, 5, 32:64].rearrange("p (t g) -> p t g", g=4)
                eg = rt[:, 5, 64:96].rearrange("p (t g) -> p t g", g=4)
                eg2 = rt[:, 5, 96:128].rearrange("p (t g) -> p t g", g=4)
                gg = rt[:, 3, 32:40]
                w1, w2, pm = rt[:, 3, 40:48], rt[:, 3, 48:56], rt[:, 3, 56:64]

                def over(v, n=4):
                    return v.unsqueeze(2).to_broadcast([P, TT, n])

                def first_max(values, top, onehot):
                    link(dve.tensor_reduce(top, values, AX, ALU.max))
                    link(dve.tensor_tensor(pr, values, over(top), ALU.is_equal))
                    link(dve.tensor_tensor(pr, pr, desc[:].unsqueeze(1).to_broadcast([P, TT, 4]), ALU.mult))
                    link(dve.tensor_reduce(pm, pr, AX, ALU.max))
                    link(dve.tensor_tensor(onehot, pr, over(pm), ALU.is_equal))

                first_max(glog, gmax, oh)
                dve.tensor_tensor(dg, glog, over(gmax), ALU.subtract).then_inc(sem("dg_ready"), 1)
                dve.tensor_copy(rt[:, 6, 0:32].rearrange("p (t g) -> p t g", g=4), oh).then_inc(sem("oh_ready"), 1)
                dve.wait_ge(sem("cnwready"), l + 1)
                pc = rt[:, 6, 32:96]
                link(dve.tensor_copy(pc, PS[:, 3, 0:64]))
                pre = pc[:, 0:32].rearrange("p (t g) -> p t g", g=4)
                cnt = pc[:, 32:64].rearrange("p (t g) -> p t g", g=4)
                tb = rt[:, 6, 96:132].rearrange("p (t g) -> p t g", g=4)
                link(dve.memset(tb[:, 0, :], 0.0))
                for t in range(TT):
                    link(dve.tensor_tensor(tb[:, t + 1, :], tb[:, t, :], cnt[:, t, :], ALU.add))
                total, nt, base = tb[:, TT, :], rt[:, 6, 132:136], rt[:, 6, 136:140]
                end = rt[:, 6, 140:144]
                link(dve.tensor_scalar(nt, total, 0.0, None, ALU.is_gt))
                for m in range(1, T // MTILE):
                    link(dve.scalar_tensor_tensor(out=nt, in0=total, scalar=float(m * MTILE), in1=nt,
                                                  op0=ALU.is_gt, op1=ALU.add))
                link(dve.tensor_copy(end, nt))
                for g in range(1, G):
                    link(dve.tensor_tensor(end[:, g:g + 1], end[:, g - 1:g], nt[:, g:g + 1], ALU.add))
                link(dve.tensor_tensor(base, end, nt, ALU.subtract))
                link(dve.tensor_scalar(base, base, float(MTILE), None, ALU.mult))
                cmp = rt[:, 7, 0:28].rearrange("p (i g) -> p i g", g=4)
                link(dve.tensor_tensor(cmp, end.unsqueeze(1).to_broadcast([P, NMT, 4]),
                                       iota[:, 0:NMT].unsqueeze(2).to_broadcast([P, NMT, 4]), ALU.is_le))
                gi = rt[:, 7, 28:28 + NMT]
                link(dve.tensor_reduce(gi, cmp, AX, ALU.add))
                dve.tensor_scalar(grp[:, 0:NMT], gi, float(G - 1), None, ALU.min).then_inc(sem("grp_ready"), 1)
                link(dve.tensor_tensor(pre, pre, tb[:, 0:TT, :], ALU.add))
                link(dve.tensor_tensor(pre, pre, base.unsqueeze(1).to_broadcast([P, TT, 4]), ALU.add))
                link(dve.tensor_tensor(pre, pre, oh, ALU.mult))
                link(dve.tensor_reduce(mm, pre, AX, ALU.add))
                link(dve.tensor_copy(slot_i[:], mm))
                sa, sb_ = rt[:, 7, 40:48], rt[:, 7, 48:56]
                saf, sbf = rt[:, 7, 56:64], rt[:, 7, 64:72]
                link(dve.tensor_single_scalar(sa.bitcast(I32), slot_i[:], 7, ALU.arith_shift_right))
                link(dve.tensor_single_scalar(sb_.bitcast(I32), slot_i[:], P - 1, ALU.bitwise_and))
                link(dve.tensor_copy(saf, sa.bitcast(I32)))
                link(dve.tensor_copy(sbf, sb_.bitcast(I32)))
                aoh = E["aoh"][:]
                link(dve.tensor_tensor(aoh, over(saf, NSUB), iota[:, 0:NSUB].unsqueeze(1).to_broadcast([P, TT, NSUB]),
                                       ALU.is_equal))
                for t in range(TT):
                    dve.tensor_scalar(E["boh"][:, t, :], iota[:], sbf[:, t:t + 1], None, ALU.is_equal)
                dve.tensor_tensor(E["avi"][:], aoh, over(tokid[:], NSUB), ALU.mult).then_inc(sem("avi_in"), 1)
                dve.wait_ge(sem("slots_ready"), l + 1)
                dve.tensor_copy(idx[:], PS[:, 4, 0:NSUB]).then_inc(sem("idx_ready"), 1)
                se = rt[:, 7, 0:128].rearrange("p (t g e) -> p t g e", t=TT, g=4)
                link(dve.tensor_tensor(se, lg[:, :, 4:20].rearrange("p t (g e) -> p t g e", g=4),
                                       oh.unsqueeze(3).to_broadcast([P, TT, 4, 4]), ALU.mult))
                link(dve.tensor_reduce(sel, se.rearrange("p t g e -> p t e g"), AX, ALU.add))
                first_max(sel, m1, o1)
                link(dve.scalar_tensor_tensor(out=sel2, in0=o1, scalar=-BIG, in1=sel, op0=ALU.mult, op1=ALU.add))
                first_max(sel2, m2, o2)
                dve.tensor_tensor(rt[:, 2, 0:8], m2, m1, ALU.subtract).then_inc(sem("dm_ready"), 1)
                dve.wait_ge(sem("eg_ready"), l + 1)
                link(dve.tensor_reduce(gg, dg, AX, ALU.add))
                dve.wait_ge(sem("em_ready"), l + 1)
                link(dve.tensor_scalar(mm, rt[:, 2, 0:8], 1.0, None, ALU.add))
                link(dve.tensor_tensor(mm, mm, gg, ALU.mult))
                link(dve.reciprocal(w1, mm))
                link(dve.tensor_tensor(w2, w1, rt[:, 2, 0:8], ALU.mult))
                link(dve.tensor_tensor(eg, o1, over(w1), ALU.mult))
                link(dve.tensor_tensor(eg2, o2, over(w2), ALU.mult))
                link(dve.tensor_tensor(eg, eg, eg2, ALU.add))
                dve.tensor_tensor(E["av"][:], aoh.unsqueeze(3).to_broadcast([P, TT, NSUB, 4]),
                                  eg.unsqueeze(2).to_broadcast([P, TT, NSUB, 4]), ALU.mult).then_inc(sem("av_in"), 1)

            def take_gates(l):
                dve.wait_ge(sem("gates_ready"), l + 1)
                link(dve.tensor_copy(gates[:], PS[:, 3, 0:NSUB * 4].rearrange("p (a v) -> p a v", v=4)))

            def moe(l):
                def x_low(i, h):
                    key = ("x", l, i, h)
                    sub, half = divmod(h, 2)
                    at_ = (slice(None), i % 2, slice(4 * half, 4 * half + 4), slice(sub * P, (sub + 1) * P))
                    out_lo(key, [(A["xtl"][at_], half_view(key), A["xth"][at_])])

                def y_out(i):
                    dve.wait_ge(sem("down_ready"), l * NSTEP + EPG * (i + 1))
                    if i >= 2:
                        dve.wait_ge(sem(f"y_stored{i % 2}"), 16 * (l * ((NMT + 1 - i % 2) // 2) + i // 2))
                    dve.tensor_copy(E["ysb"][:, i % 2, 1, :], banks(4)).then_inc(sem("y_out_v"), 1)

                advance(CH["in", l, 0], 0)
                for h in range(4):
                    x_low(0, h)
                take_gates(l)
                for s in range(NSTEP + 1):
                    i, e = divmod(s, EPG)
                    if s < NSTEP and i + 1 < NMT:
                        x_low(i + 1, e)
                    if s >= 1:
                        key = ("act", l, s - 1)
                        out_lo(key, [(A["atl"][:, (s - 1) % 2, :], bank(JOB[key] % 2)[:, 0:2 * P], A["ath"][:, (s - 1) % 2, :])])
                        if s % EPG == 1 and s > EPG:
                            y_out(s // EPG - 1)
                    if s < NSTEP:
                        advance(CH["in", l, s])
                        for sub in range(2):
                            dve.wait_ge(sem("silu_ready"), 2 * (l * NSTEP + s) + sub + 1)
                            if s >= 2 and sub == 0:
                                dve.wait_ge(xp_ready, JOB["act", l, s - 2] + 1)
                            u = PS[:, 6 + sub, HID:2 * HID]
                            dve.scalar_tensor_tensor(out=E["actm"][:, s % 2, sub, :], in0=E["sgm"][:, s % 2, sub, :],
                                                     scalar=gates[:, 2 * i + sub, e:e + 1], in1=u, op0=ALU.mult,
                                                     op1=ALU.mult).then_inc(sem("act_ready"), 1)
                    if s >= 1:
                        advance(CH["dn", l, s - 1])
                y_out(NMT - 1)
                for t in range(TT):
                    dve.wait_ge(sem(f"yg_in{t}"), 16 * (l + 1))
                    dve.tensor_tensor(X[:, t, :], X[:, t, :], A["yg"][:, t, :], ALU.add).then_inc(sem("x_sum"), 1)

            def residual(l):
                for c in range(4):
                    advance(CH["wo", l, c])
                    for t in range(TT):
                        key = ("wo", l, c, t)
                        dve.wait_ge(pj_ready, TILE[key] + 1)
                        if c == 0:
                            dve.wait_ge(sem(f"x_in{t}"), 32 + 16 * l)
                        xs = X[:, t, c * WC:(c + 1) * WC]
                        dve.tensor_tensor(xs, xs, PS[:, 2 + TILE[key] % 4, 0:WC], ALU.add).then_inc(pj_v, 1)

            norm("nmem", lambda t: E["memb"][:, t, :], MT)
            dve.wait_ge(xp_act, JOB[("cw",)] + 1)
            link(dve.tensor_scalar(gcol[:, 0:2], gcol[:, 0:2], float(MHD) ** -0.5, None, ALU.mult))
            dve.tensor_scalar(gcol[:, 4:5], gcol[:, 4:5], float(SHD) ** -0.5, None, ALU.mult).then_inc(sem("gcol_ready"), 1)
            norm("nmix0", lambda t: X[:, t, :], TT)
            for l in range(2):
                tile_out(dve, ("mem", l, 0, MT - 1))
                v = E["mkraw"][:, l].rearrange("p t (h d) -> p (t h) d", h=MH)
                for i in range(MT * MH):
                    ins = dve.tensor_tensor_reduce(out=junk[:, i % 4 * MHD:(i % 4 + 1) * MHD], in0=v[:, i, :], in1=v[:, i, :],
                                                   scale=1.0, scalar=0.0, op0=ALU.mult, op1=ALU.add, accum_out=ssq[:, i:i + 1])
                    if i % 4 == 3:
                        link(ins)
                rsqrt(rs, ssq, MT * MH, MHD)
                dve.tensor_tensor(v, v, rs[:, 0:MT * MH].unsqueeze(2).to_broadcast([P, MT * MH, MHD]), ALU.mult
                                  ).then_inc(sem("mk_ready"), 1)
                dve.wait_ge(sem("mk_ready"), l + 1)
            cin, cv = E["cin"], E["cv"]
            dve.wait_ge(xp_act, JOB["mk", 1] + 1)
            link(dve.memset(cin[:, :, 0:CW - 1], 0.0))
            extra = []

            def glu(c, h):
                s = 2 * c + h
                dve.wait_ge(sem("sig_ready"), s + 1)
                dve.tensor_tensor(cin[:, c % 2, CW - 1 + h * 512:CW - 1 + (h + 1) * 512], bank(2 + 2 * (s % 2)),
                                  C["sg"][:, s % 2, :], ALU.mult).then_inc(sem("cin_ready"), 1)

            glu_at = {0: (9, 18), 1: (8, 15), 2: (15, 21)}
            glu(0, 0)
            glu(0, 1)
            for c in range(CT):
                dve.wait_ge(sem("cin_ready"), 2 * c + 2)
                for j in range(PE_TAPS[c], CW):
                    src, tap = cin[:, c % 2, j:j + T], cw[:, c, j:j + 1]
                    if j == 0:
                        ins = dve.tensor_scalar(cv[:, c, :], src, tap, None, ALU.mult)
                    elif j == PE_TAPS[c]:
                        dve.wait_ge(sem("base_ready"), c)
                        dve.scalar_tensor_tensor(out=cv[:, c, :], in0=src, scalar=tap, in1=banks(6), op0=ALU.mult,
                                                 op1=ALU.add).then_inc(sem("base_used"), 1)
                        dve.wait_ge(sem("base_used"), c)
                        continue
                    else:
                        ins = dve.scalar_tensor_tensor(out=cv[:, c, :], in0=src, scalar=tap, in1=cv[:, c, :],
                                                       op0=ALU.mult, op1=ALU.add)
                    if j < CW - 1:
                        link(ins)
                    else:
                        ins.then_inc(sem("conv_ready"), 1)
                        dve.wait_ge(sem("conv_ready"), c + 1)
                    if c + 1 < CT and j in glu_at.get(c, (12, 20)):
                        glu(c + 1, glu_at.get(c, (12, 20)).index(j))
                    if (c, j) == HM0_AT:
                        head_norm("hm0")
                        extra = attention_steps(0)
                    if extra and (c, j) >= ATT_AT and j % 3:
                        extra.pop(0)()
            for f in extra:
                f()
            dve.wait_ge(sem("mean_ready"), 1)
            for c in range(CT):
                dve.scalar_tensor_tensor(out=cv[:, c, :], in0=banks(6), scalar=-1.0 / CC, in1=cv[:, c, :], op0=ALU.mult,
                                         op1=ALU.add).then_inc(sem("xc_ready"), 1)
            dve.wait_ge(sem("std_ready"), 1)
            for n in range(2 * CT + 2):
                if n < 2 * CT:
                    h, c = divmod(n, CT)
                    q = slice(h * 512, (h + 1) * 512)
                    dve.tensor_tensor(cv[:, c, q], cv[:, c, q], C["pt0"][:, 1, q], ALU.mult).then_inc(sem("y0_ready"), 1)
                if n >= 2:
                    h, c = divmod(n - 2, CT)
                    q = slice(h * 512, (h + 1) * 512)
                    dve.wait_ge(sem("ln_hi"), n - 1)
                    dve.tensor_tensor(A["htl_a"][:, c, q], swish(n - 2), A["hth_a"][:, c, q].bitcast(F32),
                                      ALU.subtract).then_inc(sem("ln_lo"), 1)
            residual(0)

            def ffn(l):
                norm(f"ffn{l}", lambda t: X[:, t, :], TT, lo=False)
                dispatch(l)
                moe(l)

            ffn(0)
            norm("nkv", lambda t: X[:, t, :], TT, gain=False)
            advance(CH["kv", 0, 2])
            head_norm("hk0")
            advance(CH["kv", 0, 3])
            head_norm("hk1")
            advance(CH["qs", 1, 0])
            head_norm("hm1")
            head_norm("hq0")
            for n, f in enumerate(attention_steps(1)):
                f()
                if n == 7:
                    head_norm("hq1")
            lfsum = B["lfsum"]

            def head_lo(head):
                for h in range(2):
                    dve.wait_ge(sem("sbo_hi"), 2 * head + h + 1)
                    q = slice(h * 512, (h + 1) * 512)
                    dve.tensor_tensor(A["htl_a"][:, head, q], bank(4 + 2 * (head % 2) + h), A["hth_a"][:, head, q].bitcast(F32),
                                      ALU.subtract).then_inc(sem("sbo_lo"), 1)

            for head in range(SH):
                for i, (b, q0, w, diag) in enumerate(SB_STEPS):
                    n = head * NSB + i
                    s = C["sp"][:, n % 3, 0:w]
                    dve.wait_ge(sem("l_ready"), n + 1)
                    if n >= 3:
                        dve.wait_ge(sem("r_ready"), n - 2)
                    dve.scalar_tensor_tensor(out=s, in0=PS[:, n % ZB, 0:w], scalar=0.0, in1=C["lt"][:, n % 3, 0:w],
                                             op0=ALU.max, op1=ALU.add).then_inc(sem("sp_ready"), 1)
                    dve.wait_ge(sem("sp_ready"), n + 1)
                    if i == 3 and head:
                        head_lo(head - 1)
                    if b == 0:
                        continue
                    new, old = lfsum[:, b % 2, :], lfsum[:, (b + 1) % 2, :]
                    last = [m for m in range(n) if SB_STEPS[m % NSB][0] % 2 != b % 2]
                    if last:
                        dve.wait_ge(sem("r_ready"), last[-1] + 1)
                    d = P if diag else 0
                    if diag:
                        ins = dve.tensor_copy(new[:, q0:q0 + P], s[:, 0:P])
                    if w > d:
                        ins = dve.tensor_tensor(new[:, q0 + d:q0 + w], old[:, q0 + d:q0 + w], s[:, d:w], ALU.add)
                    ins.then_inc(sem("sum_ready"), 1)
                    dve.wait_ge(sem("sum_ready"), SUMS(n))
            head_lo(SH - 1)
            residual(1)
            ffn(1)

        @block.tensor
        def _(pe):
            def job(key):
                j = JOB[key]
                if j >= 2:
                    pe.wait_ge(xp_act, j - 1)
                    if JOB_LO[j - 2]:
                        pe.wait_ge(xp_dve, JOB_LO[j - 2])
                return j % 2

            def norm_jobs(name, tiles, after=None):
                for t in range(tiles):
                    pe.wait_ge(h_ready, NT_BASE[name] + t + 1)
                    for h in range(2):
                        b = job((name, t, h))
                        for k in range(4):
                            at_ = (t % 2) * D + 4 * h + k
                            ins = pe.transpose(PS[:, b, k * P:(k + 1) * P], hb[:, at_:at_ + KT * (P - 1) + 1:KT], ident[:])
                        ins.then_inc(xp_ready, 1)
                    if after:
                        after(t)

            def chunk(n):
                pe.wait_ge(w_hi, n + 1)
                lo_made(pe, n)

            def project(kind, l, c, tiles, nk, hi, lo, halfway=None):
                n = CH[kind, l, c]
                chunk(n)
                for t in range(tiles):
                    if halfway and t == tiles // 2:
                        halfway()
                    j = TILE[kind, l, c, t]
                    if j >= 4:
                        tile_out(pe, TILES[j - 4][0])
                    tok = slice(t * P, (t + 1) * P)
                    o = PS[:, 2 + j % 4, 0:WC]
                    for k in range(nk):
                        ws = slice(k * WC, (k + 1) * WC)
                        pe.matmul(o, hi(k)[:, tok], whi(n)[:, ws], start=k == 0, stop=False)
                        pe.matmul(o, hi(k)[:, tok], wlo(n)[:, ws], start=False, stop=False)
                        ins = pe.matmul(o, lo(k)[:, tok], whi(n)[:, ws], start=False, stop=k == nk - 1)
                    ins.then_inc(pj_ready, 1)

            def head_jobs(name):
                kind, l, c = HN_CHUNK[name]
                pe.wait_ge(sem("hn_ready"), HN[name] + 1)
                raw = raw_heads(name)
                for pr in range(2):
                    for h in range(2):
                        b = job((name, pr, h))
                        for q in range(4):
                            t = 4 * h + q
                            ins = pe.transpose(PS[:, b, q * P:(q + 1) * P], raw[:, t * WC + pr * P:t * WC + (pr + 1) * P], ident[:])
                        ins.then_inc(xp_ready, 1)

            def channel_sums(c):
                if c == 0:
                    pe.wait_ge(sem("base_used"), CT - 1)
                pe.wait_ge(sem("conv_ready"), c + 1)
                for h in range(2):
                    ins = pe.matmul(bank(6 + h), ones[:], E["cv"][:, c, h * 512:(h + 1) * 512], start=c == 0, stop=c == CT - 1)
                if c == CT - 1:
                    ins.then_inc(sem("mean_ready"), 1)

            def memory_attention(l, after_first=None):
                qmT, pb, pt, nb = C[f"qmT{l}"], C[f"pb{l}"], C[f"pt{l}"], 2 - l
                on = C["on0"] if l == 0 else B["on1"]

                def scores(t):
                    if t >= 1 + l:
                        pe.wait_ge(sem("p_ready"), l * TT + t - l)
                    for pr in range(2):
                        ins = pe.matmul(bank(score_banks(l, t) + pr), qmT[:, pr, t * P:(t + 1) * P], mkT[:, l, pr, :], start=True, stop=True)
                    ins.then_inc(sem("s_ready"), 1)

                def outputs(t):
                    pe.wait_ge(xp_act, JOB["p", l, t, 1] + 1)
                    if t >= 2:
                        pe.wait_ge(sem("on_ready"), l * TT + t - 1)
                    for h in range(MH):
                        for m in range(MT):
                            q = h * MT + m
                            ins = pe.matmul(PS[:, 4 + t % 2, h * MHD:(h + 1) * MHD], pt[:, t % nb, q * P:(q + 1) * P],
                                            mv[:, l, m, h * MHD:(h + 1) * MHD], start=m == 0, stop=m == MT - 1)
                    ins.then_inc(sem("pv_ready"), 1)

                def out_job(t):
                    pe.wait_ge(sem("on_ready"), l * TT + t + 1)
                    b = job(("o", l, t))
                    for q in range(2):
                        ins = pe.transpose(PS[:, b, q * P:(q + 1) * P], on[:, t % 2, q * P:(q + 1) * P], ident[:])
                    ins.then_inc(xp_ready, 1)

                pe.wait_ge(xp_act, JOB[f"hm{l}", 1, 1] + 1)
                if l == 0:
                    pe.wait_ge(sem("cin_ready"), 2 * CT)
                else:
                    tile_out(pe, ("qs", 1, 1, TT - 1))
                scores(0)
                if after_first:
                    after_first()
                for t in range(TT):
                    if t + 1 < TT:
                        scores(t + 1)
                    pe.wait_ge(sem("p_ready"), l * TT + t + 1)
                    for h in range(2):
                        b = job(("p", l, t, h))
                        for q in range(4):
                            ins = pe.transpose(PS[:, b, q * P:(q + 1) * P], pb[:, t % nb, (4 * h + q) * P:(4 * h + q + 1) * P],
                                               ident[:])
                        ins.then_inc(xp_ready, 1)
                    if t >= 1:
                        out_job(t - 1)
                    outputs(t)
                    if l == 0 and t >= TT - CT + 1:
                        channel_sums(t - (TT - CT + 1))
                out_job(TT - 1)

            def router(l):
                def logits(t):
                    pe.wait_ge(xp_act, JOB[f"ffn{l}", t, 1] + 1)
                    if t == 0:
                        pe.wait_ge(sem("router_in"), 112 * (l + 1))
                        tile_out(pe, ("wo", l, 3, TT - 1))
                    for k in range(KT):
                        ins = pe.matmul(PS[0:20, 2 + t // 4, t % 4 * P:(t % 4 + 1) * P], rw[:, k, :], E["rT"][:, t % 2, k, :],
                                        start=k == 0, stop=k == KT - 1)
                    ins.then_inc(sem("lg_ready"), 1)

                norm_jobs(f"ffn{l}", TT, lambda t: logits(t - 1) if t else None)
                logits(TT - 1)
                for t in range(TT):
                    pe.wait_ge(sem("lg_out"), 2 * l + t // 4 + 1)
                    ins = pe.transpose(PS[:, 5, t * 20:(t + 1) * 20], logits_half(t // 4)[:, t % 4 * P:(t % 4 + 1) * P],
                                       ident[0:20, 0:20])
                ins.then_inc(sem("lt_ready"), 1)
                pe.wait_ge(sem("oh_ready"), l + 1)
                oh = E["rt"][:, 6, 0:32]
                pe.matmul(PS[:, 3, 0:32], lstrict[:], oh, start=True, stop=True)
                pe.matmul(PS[:, 3, 32:64], ones[:], oh, start=True, stop=True).then_inc(sem("cnwready"), 1)
                pe.wait_ge(sem("avi_in"), l + 1)
                for t in range(TT):
                    ins = pe.matmul(PS[:, 4, 0:NSUB], E["boh"][:, t, :], E["avi"][:, t, :], start=t == 0, stop=t == TT - 1)
                ins.then_inc(sem("slots_ready"), 1)

            def moe(l):
                def x_job(i, h):
                    sub, half = divmod(h, 2)
                    if half == 0:
                        pe.wait_ge(sem(f"xg_in{sub}"), 16 * (l * NMT + i + 1))
                    b = job(("x", l, i, h))
                    for k in range(4):
                        at_ = 4 * half + k
                        ins = pe.transpose(PS[:, b, k * P:(k + 1) * P], A["xg"][:, sub, at_:at_ + KT * (P - 1) + 1:KT], ident[:])
                    ins.then_inc(xp_ready, 1)

                def slot_gates():
                    pe.wait_ge(sem("av_in"), l + 1)
                    for t in range(TT):
                        ins = pe.matmul(PS[:, 3, 0:NSUB * EPG], E["boh"][:, t, :], E["av"][:, t].rearrange("p a v -> p (a v)"),
                                        start=t == 0, stop=t == TT - 1)
                    ins.then_inc(sem("gates_ready"), 1)

                def hidden(s):
                    i = s // EPG
                    n = CH["in", l, s]
                    if s % EPG == 0:
                        last = JOB["x", l, i, 3]
                        pe.wait_ge(xp_act, last + 1)
                        pe.wait_ge(xp_dve, JOB_LO[last])
                    chunk(n)
                    for sub in range(2):
                        if s >= 1:
                            pe.wait_ge(sem("act_ready"), 2 * (l * NSTEP + s - 1) + sub + 1)
                        o = PS[:, 6 + sub, 0:WC]
                        for k in range(KT):
                            xh = A["xth"][:, i % 2, k, sub * P:(sub + 1) * P]
                            xl = A["xtl"][:, i % 2, k, sub * P:(sub + 1) * P]
                            ws = slice(k * WC, (k + 1) * WC)
                            pe.matmul(o, xh, whi(n)[:, ws], start=k == 0, stop=False)
                            pe.matmul(o, xh, wlo(n)[:, ws], start=False, stop=False)
                            ins = pe.matmul(o, xl, whi(n)[:, ws], start=False, stop=k == KT - 1)
                        ins.then_inc(sem("hid_ready"), 1)

                def act_job(s):
                    pe.wait_ge(sem("act_ready"), 2 * (l * NSTEP + s) + 2)
                    b = job(("act", l, s))
                    for sub in range(2):
                        ins = pe.transpose(PS[:, b, sub * P:(sub + 1) * P], E["actm"][:, s % 2, sub, :], ident[:])
                    ins.then_inc(xp_ready, 1)

                def down(s):
                    i, e = divmod(s, EPG)
                    n = CH["dn", l, s]
                    chunk(n)
                    pe.wait_ge(xp_act, JOB["act", l, s] + 1)
                    pe.wait_ge(xp_dve, JOB_LO[JOB["act", l, s]])
                    if e == 0 and i >= 1:
                        pe.wait_ge(sem("y_out_a"), l * NMT + i)
                        pe.wait_ge(sem("y_out_v"), l * NMT + i)
                    for sub in range(2):
                        ah = A["ath"][:, s % 2, sub * P:(sub + 1) * P]
                        al = A["atl"][:, s % 2, sub * P:(sub + 1) * P]
                        for h in range(2):
                            o = bank(2 + 2 * sub + h)
                            ws = slice(h * 512, (h + 1) * 512)
                            pe.matmul(o, ah, whi(n)[:, ws], start=e == 0, stop=False)
                            pe.matmul(o, ah, wlo(n)[:, ws], start=False, stop=False)
                            ins = pe.matmul(o, al, whi(n)[:, ws], start=False, stop=e == EPG - 1)
                    ins.then_inc(sem("down_ready"), 1)

                pe.wait_ge(sem("idx_ready"), l + 1)
                for h in range(4):
                    x_job(0, h)
                    if h == 1:
                        slot_gates()
                for s in range(NSTEP + 1):
                    i, e = divmod(s, EPG)
                    if s < NSTEP and i + 1 < NMT:
                        x_job(i + 1, e)
                    if s >= 1:
                        act_job(s - 1)
                    if s < NSTEP:
                        hidden(s)
                    if s >= 1:
                        down(s - 1)

            pe.wait_ge(sem("consts"), 1)
            norm_jobs("nmem", MT)
            pe.wait_ge(sem("small_in"), 16 * 15)
            b = job(("cw",))
            for c in range(CT):
                pe.transpose(PS[:, b, c * (CW + 2):(c + 1) * (CW + 2)], E["cwr"][:, c * P:(c + 1) * P], ident[0:CW + 2, 0:CW + 2])
            pe.transpose(PS[:, b, 256:262], gr[0:6, :], ident[0:6, 0:6]).then_inc(xp_ready, 1)
            last = JOB["nmem", MT - 1, 1]
            pe.wait_ge(xp_act, last + 1)
            pe.wait_ge(xp_dve, JOB_LO[last])
            for n in range(4):
                project(*CHUNKS[n], MT, KT, lambda k: E["mth"][:, k, :], lambda k: E["mtl"][:, k, :])
            def key_jobs():
                for l in range(2):
                    pe.wait_ge(sem("mk_ready"), l + 1)
                    b = job(("mk", l))
                    for pr in range(2):
                        for t in range(MT):
                            ins = pe.transpose(PS[:, b, pr * MEM + t * P:pr * MEM + (t + 1) * P],
                                               E["mkraw"][:, l, t, pr * P:(pr + 1) * P], ident[:])
                    ins.then_inc(xp_ready, 1)

            def norm_done(name):
                last = JOB[name, TT - 1, 1]
                pe.wait_ge(xp_act, last + 1)
                pe.wait_ge(xp_dve, JOB_LO[last])

            norm_jobs("nmix0", TT)
            norm_done("nmix0")
            tile_out(pe, ("mem", 1, 1, MT - 1))

            def conv_base(c):
                if not PE_TAPS[c]:
                    return
                pe.wait_ge(sem("diag_ready"), c)
                pe.wait_ge(sem("cin_ready"), 2 * c + 2)
                if c >= 2:
                    pe.wait_ge(sem("base_used"), c - 1)
                for h in range(2):
                    for j in range(PE_TAPS[c]):
                        ins = pe.matmul(bank(6 + h), diagonals(c)[:, j, :], E["cin"][:, c % 2, h * 512 + j:(h + 1) * 512 + j],
                                        start=j == 0, stop=j == PE_TAPS[c] - 1)
                ins.then_inc(sem("base_ready"), 1)

            for c in range(CT):
                if c == GLU_FIRST:
                    pe.wait_ge(sem("cin_ready"), 2 * c)
                    project("qm", 0, 0, TT, KT, hth, htl)
                    tile_out(pe, ("qm", 0, 0, TT - 1))
                n = CH["glu", 0, c]
                chunk(n)
                for h in range(2):
                    s = 2 * c + h
                    if s == 1:
                        key_jobs()
                    if s >= 2:
                        pe.wait_ge(sem("cin_ready"), s - 1)
                    for g in range(2):
                        o = bank(2 + 2 * (s % 2) + g)
                        for k in range(KT):
                            ws = slice(k * WC + g * P, k * WC + (g + 1) * P)
                            q = slice(h * 512, (h + 1) * 512)
                            pe.matmul(o, whi(n)[:, ws], hth(k)[:, q], start=k == 0, stop=False)
                            pe.matmul(o, whi(n)[:, ws], htl(k)[:, q], start=False, stop=False)
                            ins = pe.matmul(o, wlo(n)[:, ws], hth(k)[:, q], start=False, stop=k == KT - 1)
                    ins.then_inc(sem("glu_ready"), 1)
                if c < CT - 1:
                    conv_base(c)
            head_jobs("hm0")
            memory_attention(0, lambda: conv_base(CT - 1))
            channel_sums(CT - 1)
            pe.wait_ge(sem("p_ready"), TT)
            for c in range(CT):
                pe.wait_ge(sem("xsq_ready"), c + 1)
                for h in range(2):
                    ins = pe.matmul(bank(2 + h), ones[:], C["pb0"][:, c % 2, h * 512:(h + 1) * 512], start=c == 0,
                                    stop=c == CT - 1)
                ins.then_inc(sem("var_used"), 1)
            pe.wait_ge(sem("ln_lo"), CT)
            pe.wait_ge(xp_dve, JOB_LO[JOB["o", 0, TT - 1]])
            for c in range(4):
                project("wo", 0, c, TT, KT, hth, htl, lambda: pe.wait_ge(sem("ln_lo"), 2 * CT))
            router(0)
            moe(0)
            norm_jobs("nkv", TT)
            norm_done("nkv")
            pe.wait_ge(sem("y_out_v"), NMT)
            pe.wait_ge(sem("y_out_a"), NMT)
            for j in range(2):
                project("kv", 0, j, TT, KT, hth, htl)
                project("kv", 0, 2 + j, TT, KT, hth, htl)
                head_jobs(f"hk{j}")
            project("qm", 1, 0, TT, KT, hth, htl)
            project("qs", 1, 0, TT, KT, hth, htl)
            head_jobs("hm1")
            project("qs", 1, 1, TT, KT, hth, htl)
            head_jobs("hq0")
            memory_attention(1)
            head_jobs("hq1")
            pe.wait_ge(xp_act, JOB["hq1", 1, 1] + 1)
            kT, V, qT = E["kT"], E["V"], C["qT"]
            pe.wait_ge(sem("on_ready"), 2 * TT)
            pe.wait_ge(xp_act, JOB["o", 1, TT - 1] + 1)
            pe.wait_ge(xp_dve, JOB_LO[JOB["o", 1, TT - 1]])

            def logits(n):
                head, i = divmod(n, NSB)
                b, q0, w, diag = SB_STEPS[i]
                if n >= ZB:
                    pe.wait_ge(sem("wgt_ready"), n - ZB + 1)
                ins = pe.matmul(PS[:, n % ZB, 0:w], kT[:, head, b * P:(b + 1) * P], qT[:, head, q0:q0 + w], start=True,
                                stop=not diag, skip_group_check=True)
                if diag:
                    ins = pe.matmul(PS[:, n % ZB, 0:P], ident[:], negm[:], start=False, stop=True, skip_group_check=True)
                ins.then_inc(sem("z_ready"), 1)

            def remainders(n):
                head, i = divmod(n, NSB)
                b, q0, w, diag = SB_STEPS[i]
                pe.wait_ge(sem("sp_ready"), n + 1)
                d = P if diag else 0
                ins = pe.matmul(PS[:, n % ZB, 0:w], nuinc[:], C["sp"][:, n % 3, 0:w], start=False, stop=w == d,
                                skip_group_check=True)
                if w > d:
                    before = [m for m in range(head * NSB, n) if SB_STEPS[m % NSB][0] == b + 1 and
                              SB_STEPS[m % NSB][1] // 512 == q0 // 512]
                    pe.wait_ge(sem("sum_ready"), SUMS(before[-1]))
                    ins = pe.matmul(PS[:, n % ZB, d:w], nones[:], B["lfsum"][:, (b + 1) % 2, q0 + d:q0 + w], start=False,
                                    stop=True, skip_group_check=True)
                ins.then_inc(sem("r_ready"), 1)

            def values(n):
                head, i = divmod(n, NSB)
                b, q0, w, diag = SB_STEPS[i]
                h = q0 // 512
                pe.wait_ge(sem("wgt_ready"), n + 1)
                firsts = [j for j in range(NSB) if SB_STEPS[j][1] // 512 == h]
                if i == 0 and head >= 2:
                    pe.wait_ge(sem("sbo_lo"), 2 * (head - 1))
                c0 = q0 - h * 512
                ins = pe.matmul(PS[:, 4 + 2 * (head % 2) + h, c0:c0 + w], V[:, b, head * SHD:(head + 1) * SHD],
                                B["wgt"][:, n % 2, 0:w], start=i == firsts[0], stop=i == firsts[-1], skip_group_check=True)
                ins.then_inc(sem("av_ready"), 1)

            total = SH * NSB
            for n in range(total + 3):
                if n < total:
                    logits(n)
                if 2 <= n <= total + 1:
                    values(n - 2)
                if 1 <= n <= total:
                    remainders(n - 1)
            pe.wait_ge(sem("sbo_lo"), 2 * SH)
            for c in range(4):
                project("wo", 1, c, TT, 6, hth, htl)
            router(1)
            moe(1)


def SUMS(n):
    head, i = divmod(n, NSB)
    with_sum = [b > 0 for b, _, _, _ in SB_STEPS]
    return head * sum(with_sum) + sum(with_sum[:i + 1])


_INS = ["x", "mem", "mem_norm_g", "mix_norm_g", "ffn_norm_g", "w_in_a", "conv_w", "conv_ln_g", "conv_ln_b", "w_out_a",
        "w_in_b", "sb_q_norm_g", "w_out_b", "kv_norm_g", "w_kv", "sb_k_norm_g", "w_mem_kv", "mem_q_norm_g",
        "mem_k_norm_g", "router_g_w", "router_g_b", "router_e_w", "router_e_b", "moe_w_in", "moe_w_down"]


def kernel(**inputs):
    import concourse.bacc as bacc
    from concourse.bass_utils import run_bass_kernel_spmd

    nc = bacc.Bacc("TRN2", target_bir_lowering=False, num_devices=1)
    arrays, args = {}, {}
    for name in _INS:
        v = np.ascontiguousarray(inputs[name])
        arrays[f"in_{name}"] = v
        args[name] = nc.dram_tensor(f"in_{name}", v.shape, mybir.dt.from_np(v.dtype), kind="ExternalInput").ap()
    out = nc.dram_tensor("out_0", (1, T, D), F32, kind="ExternalOutput").ap()
    trunk(nc, args, out)
    r = run_bass_kernel_spmd(nc, [arrays], core_ids=[0])
    return r.results[0]["out_0"]
```
